# Optimizing a Trainium2 kernel written in Bass

```python
import math
import jax, jax.numpy as jnp
from jax import lax
import numpy as np

D_MODEL = 1024
BATCH = 1
SEQ = 512
DEPTH = 1
DEC_BATCH = 8
DEC_SEQ = 8
PAST_LEN = 1024
PAGE_SIZE = 128

SSM_WIDTH = D_MODEL // 2
SSM_GROUP = 16
SSM_GROUPS = SSM_WIDTH // SSM_GROUP
SSM_STATE = 64
N_HEADS = 8
N_KV_HEADS = 2
Q_PER_KV = N_HEADS // N_KV_HEADS
HEAD_DIM = 64
ATTN_WIDTH = N_HEADS * HEAD_DIM
KV_WIDTH = N_KV_HEADS * HEAD_DIM
WINDOW = 128
ROPE_DIM = HEAD_DIM // 4
ROPE_THETA = 500000.0
SPLITS = [SSM_WIDTH, SSM_WIDTH + ATTN_WIDTH, SSM_WIDTH + ATTN_WIDTH + KV_WIDTH,
          SSM_WIDTH + ATTN_WIDTH + 2 * KV_WIDTH, SSM_WIDTH + ATTN_WIDTH + 2 * KV_WIDTH + D_MODEL]
IN_WIDTH = SSM_WIDTH + ATTN_WIDTH + 2 * KV_WIDTH + 2 * D_MODEL
PEER_HEADS = 8
PEER_KEYS = 128
PEER_EXPERTS = PEER_KEYS * PEER_KEYS
PEER_KEY_DIM = 128
PEER_HALF = PEER_KEY_DIM // 2
PEER_TOPK = 16
PEER_BLOCK = 128
ALPHA = (2.0 * DEPTH) ** 0.25
BETA = (8.0 * DEPTH) ** -0.25
LN_EPS = 1e-5
NEG_INF = -1e30

kernel_name = "hybrid_s5_swa_peer_deepnorm_step"

def layer_norm(x, g, b):
    xf = x.astype(jnp.float32)
    mu = jnp.mean(xf, axis=-1, keepdims=True)
    var = jnp.mean(jnp.square(xf - mu), axis=-1, keepdims=True)
    return ((xf - mu) * lax.rsqrt(var + LN_EPS) * g.astype(jnp.float32) + b.astype(jnp.float32)).astype(x.dtype)

def partial_rope(x, pos):
    freqs = ROPE_THETA ** (-jnp.arange(0, ROPE_DIM, 2, dtype=jnp.float32) / ROPE_DIM)
    ang = pos.astype(jnp.float32)[:, None] * freqs[None, :]
    cos = jnp.cos(ang)[:, None, :]
    sin = jnp.sin(ang)[:, None, :]
    xr = x[..., :ROPE_DIM].astype(jnp.float32)
    x1, x2 = xr[..., :ROPE_DIM // 2], xr[..., ROPE_DIM // 2:]
    rot = jnp.concatenate([x1 * cos - x2 * sin, x2 * cos + x1 * sin], axis=-1)
    return jnp.concatenate([rot.astype(x.dtype), x[..., ROPE_DIM:]], axis=-1)

def s5_scan(u, h0_re, h0_im, a_re, a_im, log_dt, b_re, b_im, c_re, c_im, d):
    f32 = jnp.float32
    bsz, t = u.shape[0], u.shape[1]
    dt = jnp.exp(log_dt.astype(f32))[:, None]
    a = lax.complex(a_re.astype(f32), a_im.astype(f32))
    a_bar = jnp.exp(a * dt)
    b = lax.complex(b_re.astype(f32), b_im.astype(f32))
    b_bar = ((a_bar - 1.0) / a)[..., None] * b
    ug = u.astype(f32).reshape(bsz, t, SSM_GROUPS, SSM_GROUP).astype(jnp.complex64)
    bu = jnp.einsum('gpc,btgc->btgp', b_bar, ug)
    h0 = lax.complex(h0_re.astype(f32), h0_im.astype(f32))
    bu = bu.at[:, 0].add(a_bar[None] * h0)
    decay = jnp.broadcast_to(a_bar, bu.shape)

    def combine(l, r):
        return (r[0] * l[0], r[0] * l[1] + r[1])

    _, hs = lax.associative_scan(combine, (decay, bu), axis=1)
    c = lax.complex(c_re.astype(f32), c_im.astype(f32))
    y = jnp.real(jnp.einsum('gcp,btgp->btgc', c, hs)).reshape(bsz, t, SSM_WIDTH)
    y = y + d.astype(f32) * u.astype(f32)
    h_last = hs[:, -1]
    return y.astype(u.dtype), jnp.real(h_last), jnp.imag(h_last)

def sink_attention(q, k, v, mask, sinks):
    f32 = jnp.float32
    s = jnp.einsum('bnqkgd,bnskd->bnkgqs', q.astype(f32), k.astype(f32)) * (HEAD_DIM ** -0.5)
    s = jnp.where(mask[None, :, None, None], s, NEG_INF)
    sink = jnp.broadcast_to(sinks.astype(f32).reshape(N_KV_HEADS, Q_PER_KV)[None, None, :, :, None, None],
                            s.shape[:-1] + (1,))
    p = jax.nn.softmax(jnp.concatenate([s, sink], axis=-1), axis=-1)[..., :-1]
    o = jnp.einsum('bnkgqs,bnskd->bnqkgd', p, v.astype(f32))
    return o.astype(q.dtype)

def window_attention_prompt(q, k, v, sinks):
    bsz, t = q.shape[0], q.shape[1]
    nb = t // WINDOW
    qb = q.reshape(bsz, nb, WINDOW, N_KV_HEADS, Q_PER_KV, HEAD_DIM)
    pad = ((0, 0), (WINDOW, 0), (0, 0), (0, 0))
    kp = jnp.pad(k, pad).reshape(bsz, nb + 1, WINDOW, N_KV_HEADS, HEAD_DIM)
    vp = jnp.pad(v, pad).reshape(bsz, nb + 1, WINDOW, N_KV_HEADS, HEAD_DIM)
    kb = jnp.concatenate([kp[:, :-1], kp[:, 1:]], axis=2)
    vb = jnp.concatenate([vp[:, :-1], vp[:, 1:]], axis=2)
    qi = jnp.arange(WINDOW)[:, None]
    sj = jnp.arange(2 * WINDOW)[None, :]
    rel = WINDOW + qi - sj
    band = (rel >= 0) & (rel < WINDOW)
    valid = (jnp.arange(nb)[:, None, None] > 0) | (sj[None] >= WINDOW)
    mask = band[None] & valid
    o = sink_attention(qb, kb, vb, mask, sinks)
    return o.reshape(bsz, t, ATTN_WIDTH), k[:, t - WINDOW:], v[:, t - WINDOW:]

def window_attention_sample(q, k_new, v_new, k_buf, v_buf, sinks):
    bsz, s = q.shape[0], q.shape[1]
    kk = jnp.concatenate([k_buf.astype(k_new.dtype), k_new], axis=1)
    vv = jnp.concatenate([v_buf.astype(v_new.dtype), v_new], axis=1)
    rel = (jnp.arange(s)[:, None] + WINDOW) - jnp.arange(WINDOW + s)[None, :]
    mask = (rel >= 0) & (rel < WINDOW)
    qb = q.reshape(bsz, 1, s, N_KV_HEADS, Q_PER_KV, HEAD_DIM)
    o = sink_attention(qb, kk[:, None], vv[:, None], mask[None], sinks)
    return o.reshape(bsz, s, ATTN_WIDTH), kk[:, s:], vv[:, s:]

def token_mixer(x, pos, h0_re, h0_im, k_buf, v_buf, p):
    bsz, t = x.shape[0], x.shape[1]
    z = x @ p['w_in'] + p['b_in']
    u, q, k, v, g_ssm, g_attn = jnp.split(z, SPLITS, axis=-1)
    y, h_re, h_im = s5_scan(u, h0_re, h0_im, p['ssm_a_re'], p['ssm_a_im'], p['ssm_log_dt'],
                            p['ssm_b_re'], p['ssm_b_im'], p['ssm_c_re'], p['ssm_c_im'], p['ssm_d'])
    hg = jax.nn.gelu(y, approximate=False)
    ga, gb = jnp.split(hg @ p['w_glu'] + p['b_glu'], 2, axis=-1)
    ssm_branch = ga * jax.nn.sigmoid(gb)
    q = partial_rope(q.reshape(bsz, t, N_HEADS, HEAD_DIM), pos)
    k = partial_rope(k.reshape(bsz, t, N_KV_HEADS, HEAD_DIM), pos)
    v = v.reshape(bsz, t, N_KV_HEADS, HEAD_DIM)
    if k_buf is None:
        o, k_win, v_win = window_attention_prompt(q, k, v, p['attn_sinks'])
    else:
        o, k_win, v_win = window_attention_sample(q, k, v, k_buf, v_buf, p['attn_sinks'])
    attn_branch = o @ p['w_attn_up']
    merged = jax.nn.sigmoid(g_ssm) * ssm_branch + jax.nn.sigmoid(g_attn) * attn_branch
    return merged @ p['w_out'], k_win, v_win, h_re, h_im

def peer(x, p):
    f32 = jnp.float32
    bsz, t, dm = x.shape
    xf = x.reshape(-1, dm)
    n = xf.shape[0]
    q = (xf @ p['peer_wq']).astype(f32).reshape(n, PEER_HEADS, 2, PEER_HALF)
    s1 = jnp.einsum('nhd,hkd->nhk', q[:, :, 0], p['peer_k1'].astype(f32))
    s2 = jnp.einsum('nhd,hkd->nhk', q[:, :, 1], p['peer_k2'].astype(f32))
    v1, i1 = lax.top_k(s1, PEER_TOPK)
    v2, i2 = lax.top_k(s2, PEER_TOPK)
    cand = (v1[..., :, None] + v2[..., None, :]).reshape(n, PEER_HEADS, PEER_TOPK * PEER_TOPK)
    cidx = (i1[..., :, None] * PEER_KEYS + i2[..., None, :]).reshape(n, PEER_HEADS, PEER_TOPK * PEER_TOPK)
    sc, sel = lax.top_k(cand, PEER_TOPK)
    idx = jnp.take_along_axis(cidx, sel, axis=-1)
    gate = jax.nn.softmax(sc, axis=-1)
    n_pad = (-n) % PEER_BLOCK
    nblk = (n + n_pad) // PEER_BLOCK
    xb = jnp.pad(xf, ((0, n_pad), (0, 0))).reshape(nblk, PEER_BLOCK, dm)
    ib = jnp.pad(idx, ((0, n_pad), (0, 0), (0, 0))).reshape(nblk, PEER_BLOCK, PEER_HEADS, PEER_TOPK)
    gbk = jnp.pad(gate, ((0, n_pad), (0, 0), (0, 0))).reshape(nblk, PEER_BLOCK, PEER_HEADS, PEER_TOPK)
    peer_u, peer_v = p['peer_u'], p['peer_v']

    def expert_block(args):
        xi, ii, gi = args
        h = jnp.einsum('nhkd,nd->nhk', peer_u[ii], xi)
        a = jax.nn.gelu(h.astype(f32), approximate=False) * gi
        return jnp.einsum('nhk,nhkd->nd', a.astype(x.dtype), peer_v[ii])

    out = lax.map(expert_block, (xb, ib, gbk)).reshape(-1, dm)[:n]
    return out.reshape(bsz, t, dm).astype(x.dtype)

def decoder_layer(x, pos, h0_re, h0_im, k_buf, v_buf, p):
    mix, k_win, v_win, h_re, h_im = token_mixer(x, pos, h0_re, h0_im, k_buf, v_buf, p)
    x1 = layer_norm(ALPHA * x + mix, p['ln1_g'], p['ln1_b'])
    x2 = layer_norm(ALPHA * x1 + peer(x1, p), p['ln2_g'], p['ln2_b'])
    return x2, k_win, v_win, h_re, h_im

def setup_inputs(seed: int = 0) -> dict:
    key = jax.random.key(seed)
    ks = jax.random.split(key, 32)
    nrm = lambda k, shape, s: jax.random.normal(k, shape, jnp.float32) * s
    L = DEPTH
    a_im_base = math.pi * jnp.arange(SSM_STATE, dtype=jnp.float32)
    return {
        'x_prompt': nrm(ks[0], (BATCH, SEQ, D_MODEL), 1.0),
        'x_sample': nrm(ks[1], (DEC_BATCH, DEC_SEQ, D_MODEL), 1.0),
        'cache_k_win': nrm(ks[2], (L, DEC_BATCH, WINDOW, N_KV_HEADS, HEAD_DIM), 1.0),
        'cache_v_win': nrm(ks[3], (L, DEC_BATCH, WINDOW, N_KV_HEADS, HEAD_DIM), 1.0),
        'state_ssm_re': nrm(ks[4], (L, DEC_BATCH, SSM_GROUPS, SSM_STATE), 0.1),
        'state_ssm_im': nrm(ks[5], (L, DEC_BATCH, SSM_GROUPS, SSM_STATE), 0.1),
        'w_in': nrm(ks[6], (L, D_MODEL, IN_WIDTH), D_MODEL ** -0.5),
        'b_in': nrm(ks[7], (L, IN_WIDTH), 0.01),
        'ssm_a_re': -0.5 + nrm(ks[8], (L, SSM_GROUPS, SSM_STATE), 0.01),
        'ssm_a_im': a_im_base + nrm(ks[9], (L, SSM_GROUPS, SSM_STATE), 0.01),
        'ssm_log_dt': jax.random.uniform(ks[10], (L, SSM_GROUPS), jnp.float32, math.log(1e-3), math.log(1e-1)),
        'ssm_b_re': nrm(ks[11], (L, SSM_GROUPS, SSM_STATE, SSM_GROUP), (2.0 * SSM_GROUP) ** -0.5),
        'ssm_b_im': nrm(ks[12], (L, SSM_GROUPS, SSM_STATE, SSM_GROUP), (2.0 * SSM_GROUP) ** -0.5),
        'ssm_c_re': nrm(ks[13], (L, SSM_GROUPS, SSM_GROUP, SSM_STATE), SSM_STATE ** -0.5),
        'ssm_c_im': nrm(ks[14], (L, SSM_GROUPS, SSM_GROUP, SSM_STATE), SSM_STATE ** -0.5),
        'ssm_d': nrm(ks[15], (L, SSM_WIDTH), 1.0),
        'w_glu': nrm(ks[16], (L, SSM_WIDTH, 2 * D_MODEL), SSM_WIDTH ** -0.5),
        'b_glu': nrm(ks[17], (L, 2 * D_MODEL), 0.01),
        'attn_sinks': nrm(ks[18], (L, N_HEADS), 0.5),
        'w_attn_up': nrm(ks[19], (L, ATTN_WIDTH, D_MODEL), ATTN_WIDTH ** -0.5),
        'w_out': nrm(ks[20], (L, D_MODEL, D_MODEL), BETA * D_MODEL ** -0.5),
        'ln1_g': 1.0 + nrm(ks[21], (L, D_MODEL), 0.01),
        'ln1_b': nrm(ks[22], (L, D_MODEL), 0.01),
        'peer_wq': nrm(ks[23], (L, D_MODEL, PEER_HEADS * PEER_KEY_DIM), D_MODEL ** -0.5),
        'peer_k1': nrm(ks[24], (L, PEER_HEADS, PEER_KEYS, PEER_HALF), PEER_HALF ** -0.5),
        'peer_k2': nrm(ks[25], (L, PEER_HEADS, PEER_KEYS, PEER_HALF), PEER_HALF ** -0.5),
        'peer_u': nrm(ks[26], (L, PEER_EXPERTS, D_MODEL), D_MODEL ** -0.5),
        'peer_v': nrm(ks[27], (L, PEER_EXPERTS, D_MODEL), BETA * D_MODEL ** -0.5),
        'ln2_g': 1.0 + nrm(ks[28], (L, D_MODEL), 0.01),
        'ln2_b': nrm(ks[29], (L, D_MODEL), 0.01),
    }

def reference(x_prompt, x_sample, cache_k_win, cache_v_win, state_ssm_re, state_ssm_im,
              w_in, b_in, ssm_a_re, ssm_a_im, ssm_log_dt, ssm_b_re, ssm_b_im, ssm_c_re, ssm_c_im,
              ssm_d, w_glu, b_glu, attn_sinks, w_attn_up, w_out, ln1_g, ln1_b,
              peer_wq, peer_k1, peer_k2, peer_u, peer_v, ln2_g, ln2_b):
    pos_prompt = jnp.arange(SEQ, dtype=jnp.int32)
    pos_sample = PAST_LEN + jnp.arange(DEC_SEQ, dtype=jnp.int32)
    zero_state = jnp.zeros((BATCH, SSM_GROUPS, SSM_STATE), jnp.float32)
    xp, xs = x_prompt, x_sample
    kwp, vwp, hrp, hip, kws, vws, hrs, his = [], [], [], [], [], [], [], []
    for l in range(DEPTH):
        p = {
            'w_in': w_in[l], 'b_in': b_in[l], 'ssm_a_re': ssm_a_re[l], 'ssm_a_im': ssm_a_im[l],
            'ssm_log_dt': ssm_log_dt[l], 'ssm_b_re': ssm_b_re[l], 'ssm_b_im': ssm_b_im[l],
            'ssm_c_re': ssm_c_re[l], 'ssm_c_im': ssm_c_im[l], 'ssm_d': ssm_d[l],
            'w_glu': w_glu[l], 'b_glu': b_glu[l], 'attn_sinks': attn_sinks[l],
            'w_attn_up': w_attn_up[l], 'w_out': w_out[l], 'ln1_g': ln1_g[l], 'ln1_b': ln1_b[l],
            'peer_wq': peer_wq[l], 'peer_k1': peer_k1[l], 'peer_k2': peer_k2[l],
            'peer_u': peer_u[l], 'peer_v': peer_v[l], 'ln2_g': ln2_g[l], 'ln2_b': ln2_b[l],
        }
        xp, kw, vw, hr, hi = decoder_layer(xp, pos_prompt, zero_state, zero_state, None, None, p)
        kwp.append(kw); vwp.append(vw); hrp.append(hr); hip.append(hi)
        xs, kw, vw, hr, hi = decoder_layer(xs, pos_sample, state_ssm_re[l], state_ssm_im[l],
                                           cache_k_win[l], cache_v_win[l], p)
        kws.append(kw); vws.append(vw); hrs.append(hr); his.append(hi)
    return (xp, xs, jnp.stack(kwp), jnp.stack(vwp), jnp.stack(hrp), jnp.stack(hip),
            jnp.stack(kws), jnp.stack(vws), jnp.stack(hrs), jnp.stack(his))


_drawn_inputs = setup_inputs


def setup_inputs(seed=0):
    import zlib

    import numpy as np

    out = dict(_drawn_inputs(seed))
    spreads = {}
    factors = {'ssm_a_re': 4.065,
     'ssm_c_re': 6.129,
     'ssm_c_im': 6.183,
     'b_glu': 8.0,
     'attn_sinks': 8.0,
     'ln1_g': 5.469,
     'ln1_b': 5.636,
     'peer_wq': 7.484,
     'peer_k1': 7.653,
     'peer_k2': 7.617,
     'peer_u': 8.0,
     'peer_v': 7.44,
     'ln2_g': 5.48,
     'ln2_b': 5.86}
    for name, (base, spread) in spreads.items():
        noise = np.random.default_rng([zlib.crc32(name.encode()), seed]).standard_normal(out[name].shape)
        drawn = base * np.exp(spread * noise) if base else spread * noise
        out[name] = __import__('jax').numpy.asarray(drawn.astype(out[name].dtype))
    for name, factor in factors.items():
        out[name] = (out[name] * factor).astype(out[name].dtype)
    return out
```

```python
import math
from contextlib import ExitStack

import numpy as np

import concourse.bass as bass
from concourse import mybir

F32, U32 = mybir.dt.float32, mybir.dt.uint32
ALU, ACT = mybir.AluOpType, mybir.ActivationFunctionType
AX = mybir.AxisListType.X

DM, SEQ, NSEQ, STEP, PAST = 1024, 512, 8, 8, 1024
SSM, G, GC, NS = 512, 32, 16, 64
NH, NKV, HD, WIN, ROPE = 8, 2, 64, 128, 16
HP = NH // NKV
NE, KEYS, TOPK, HALF = 16384, 128, 16, 64
TOK = NSEQ * STEP + SEQ
CH = TOK // STEP
GP = G // 2
KT = DM // 128
ALPHA, EPS, NEG = 2.0 ** 0.25, 1e-5, -1e30
TILES = [(0, 64)] + [(64 + 128 * j, 128) for j in range(4)]
GROUPS = [[0, 1], [2, 3, 4]]
GC0 = [(0, 192), (192, 384)]
CHUNKS = [(0, 24), (24, 48)]
ORDER = [1, 0, 2, 3, 4]
RING = 8
GR1, GR2 = 4, 10
V_SHARE = {1: [2] * 7 + [5] * 9, 0: [5] * 2 + [3] * 4 + [1] * 2}
DR = 8
CHK = 4

_SMALL = [("ident", 128), ("fold", 64), ("are", GP), ("aim", GP), ("ldt", GP), ("bb", 2 * GP * GC),
          ("cc", 2 * GP * GC), ("k12", NH * KEYS), ("maskp", 2 * WIN), ("masks", 2 * (WIN + 64)),
          ("rope", 5 * ROPE), ("h0", 2 * GP * NSEQ), ("bu", 4), ("bgs", 8), ("bga", 8), ("bglu", 16),
          ("sinkp", NH), ("sinks", NKV), ("dskip", G * GC), ("iota", TOPK), ("bqkv", 768)]
SM, _c = {}, 0
for _n, _w in _SMALL:
    SM[_n] = (_c, _c + _w)
    _c += _w
SMC = _c


def n_slots(t):
    return 64 if t == 0 else 128


def schedule():
    s = [("tables",), ("u",), ("ut",), ("uc",), ("qkv", 0), ("qkv", 1), ("turn", 0), ("turn", 1), ("wt",), ("k",), ("ws",),
         ("rec", 0), ("ss",), ("gates", 0), ("gates", 1), ("pvs",), ("s", 0, 0), ("gates", 2), ("gates", 3), ("pv", 0, 0),
         ("s", 0, 1), ("gates", 4), ("gates", 5), ("pv", 0, 1), ("gates", 6), ("gates", 7), ("y", 0), ("ht", 0), ("rec", 1)]
    s += [("merge", 0, m) for m in range(8)]
    s += [("y", 1), ("ht", 1), ("wo", 0), ("wo", 1), ("xt", 0), ("xt", 1)] + [("wq", 0, h) for h in range(8)]
    s += [("sc", 1, 0), ("sc", 1, 1)] + [("top", 1, h) for h in range(8)] + [("choose", 1, i) for i in range(3)]
    tops = [[("sc", 0, 0), ("top", 0, 0)]] + [[("top", 0, h)] for h in (1, 2)] + [[("top", 0, 3), ("sc", 0, 1)]]
    tops += [[("top", 0, h)] for h in (4, 5, 6, 7)] + [[("choose", 0, 0)], [("choose", 0, 1)], [("choose", 0, 2), ("fold",)]]
    mix = [[("qkv", 2)], [("qkv", 3)], [("qkv", 4)], [("turn", 2), ("turn", 3), ("turn", 4), ("s", 1, 0)]]
    parts = [(j, kv) for j in range(1, 4) for kv in range(2)]
    for n, (j, kv) in enumerate(parts):
        mix.append([("pv", j, kv)] + ([("s", *parts[n + 1])] if n + 1 < len(parts) else []))
    for m in range(8):
        mix += [[("merge", 1, m)], []]
    mix += [[("wo", 2)], [("wo", 3), ("xt", 2)], [("wo", 4), ("xt", 3)], [("xt", 4), ("wq", 1, 0)]]
    mix += [[("wq", 1, h)] for h in range(1, 8)]
    mix += [[("sc", 2, 0), ("sc", 2, 1), ("top", 2, 0)]] + [[("top", 2, h)] for h in range(1, 8)] + [[("choose", 2, i)] for i in range(3)]
    b = []
    for n, entry in enumerate(mix):
        if tops and (n < 4 or not entry):
            b.append(tops.pop(0))
        if entry:
            b.append(entry)
    steps = [("peer", t, c) for t in ORDER[:2] for c in range(n_slots(t) // CHK)]
    per, at = len(b) / len(steps), 0.0
    for t in ORDER:
        n = n_slots(t) // CHK
        nxt = [("sc", t + 1, 0), ("sc", t + 1, 1)] + [("top", t + 1, h) for h in range(8)] + [("choose", t + 1, i) for i in range(3)]
        for c in range(n):
            s.append(("peer", t, c))
            if c == 0 and t != ORDER[0]:
                s.append(("final", ORDER[ORDER.index(t) - 1]))
            if t in ORDER[:2]:
                at += per
                while b and at >= 1 - 1e-9:
                    s += b.pop(0)
                    at -= 1
            elif t < 4 and c >= 2 and c % 2 == 0 and nxt:
                s.append(nxt.pop(0))
        s.append(("last", t))
        if t == ORDER[1]:
            for x in b:
                s += x
    s.append(("final", ORDER[-1]))
    return s


def mixer_first(items):
    out, held = [], None
    for item in items:
        if item[0] in ("peer", "last") and held:
            out.append(held)
            held = None
        if item[0] == "peer":
            held = item
            out.append(("before", *item[1:]))
        else:
            out.append(item)
    return out + ([held] if held else [])


def item_jobs(item):
    k, a, ad = item[0], item[1:], "AD"
    if k == "u":
        return [(("u", c, m), "A", [("u", m)]) for c in range(2) for m in range(4)]
    if k in ("ut", "uc"):
        return [((k, i), "A", []) for i in range(8)]
    if k in ("wt", "k", "ws"):
        return [((k, i // 4, i % 4), ad[i % 2], []) for i in range(8)]
    if k == "y":
        return [(("y", a[0], i // 4, i % 4), "A", []) for i in range(8)]
    if k == "ht":
        return [(("ht", a[0], i // 2, i % 2), "A", []) for i in range(8)]
    if k == "qkv":
        g = a[0] > 1
        return [(("q", a[0]), "D", [(g, "q", i) for i in range(4)]), (("kv", a[0]), "D", [(g, "kv", i) for i in range(2)])]
    if k == "turn":
        return [(("qt", a[0]), "A", []), (("kt", a[0]), "A", [])]
    if k == "ss":
        return [(("ss", i // 2, i % 2), "D", []) for i in range(4)]
    if k == "pvs":
        return [(("spc",), "A", []), (("spn",), "A", []), (("so",), "D", [])]
    if k == "s":
        return [(("s", *a, hf), "D", []) for hf in range(2)]
    if k == "pv":
        return [(("pt", *a, i), "A", []) for i in range(2)] + [(("o", *a), "D", [])]
    if k == "gates":
        return [((w, 0, a[0]), "A", [(0, w, a[0])]) for w in ("gs", "ga")]
    if k == "merge":
        g, m = a
        jobs = [((w, g, m), "A", [(g, w, m)]) for w in ("gs", "ga")] if g else []
        return jobs + [(("gb", g, m), "A", [(g, "glu", m)]), (("gl", g, m), "D", [(g, "glu", m)]), (("up", g, m), "D", [(g, "up", m // 2)])]
    if k == "wo":
        return [(("wo", a[0], hf), "D", [(a[0] > 1, "wo", i) for i in range(8)]) for hf in range(2)]
    if k == "xt":
        return [(("xt", a[0], hf), "A", []) for hf in range(2)]
    if k == "wq":
        return [(("wq", *a), ad[a[1] % 2], [(a[0], "wq", a[1])])]
    if k == "sc":
        return [(("sc", a[0], side, a[1]), "S", []) for side in range(2)]
    if k == "last":
        return [(("po", a[0], hf), "D", []) for hf in range(2)]
    return []


class Plan:

    def __init__(self):
        self.items = schedule()
        self.filled, self.drained, self.before, self.bank = {}, {}, {}, {}
        self.passed, self.index, self.pieces, self.last_use = {}, {}, [], {}
        window = self.items.index(("peer", ORDER[0], 0))
        scores_read = 0
        last, n, counts, turn, kinds = {}, 0, {"D": 0, "A": 0, "S": 0}, 0, {}
        for at, item in enumerate(self.items):
            kinds[item[0]] = kinds.get(item[0], 0) + 1
            self.index[item] = kinds[item[0]]
            for key, who, pieces in item_jobs(item):
                if key[0] == "po":
                    bank = 6 + key[2]
                elif key[0] == "sc":
                    bank = key[2] + (4 if key[3] == 0 or key[1] == 0 else 6 if key[1] == 1 else 2)
                elif at < window:
                    bank, turn = turn % 8, turn + 1
                else:
                    bank, turn = turn % 4, turn + 1
                n += key[0] != "po"
                counts[who] += 1
                self.filled[key], self.drained[key], self.bank[key] = n, (who, counts[who]), bank
                self.before[key] = last.get(bank)
                last[bank] = (who, counts[who])
                for p in pieces:
                    p = (int(p[0]), *p[1:]) if len(p) == 3 else (0, *p)
                    if p not in self.last_use:
                        self.pieces.append(p)
                    self.last_use[p] = key
            if item[0] == "top" and item[2] % 4 == 3:
                scores_read += 2
            self.passed[item] = (n, counts["D"], counts["A"], scores_read)


def hybrid_step(nc, io):
    plan = Plan()
    pieces = plan.pieces
    piece_no = {p: i for i, p in enumerate(pieces)}

    ctx = ExitStack()
    with ctx:
        def sb(name, shape, dt=F32):
            return ctx.enter_context(nc.sbuf_tensor(name, shape, dt))

        def sem(name):
            return ctx.enter_context(nc.semaphore(name))

        wring = sb("wring", [128, RING, 1024])
        small = sb("small", [128, SMC])
        xT = sb("xT", [128, KT, TOK])
        hgT = sb("hgT", [128, 4, TOK])
        R = sb("region", [128, 31944])
        fin = sb("fin", [128, 2, GP, 1 + NSEQ])
        cx = sb("cx", [128, 10, 2, GP])
        stat = sb("stat", [128, 80])
        Bb = sb("Bbar", [128, 2, GP, GC])
        pw = sb("powers", [128, 2, GP, 9])
        a8 = sb("a8", [128, 2, 2, GP])

        def s(name, *dims):
            a, b = SM[name]
            v = small[:, a:b]
            if len(dims) == 2:
                v = v.rearrange("p (a b) -> p a b", a=dims[0])
            if len(dims) == 3:
                v = v.rearrange("p (a b c) -> p a b c", a=dims[0], b=dims[1])
            return v

        def view(at, *dims):
            v = R[:, at:at + math.prod(dims)]
            if len(dims) == 2:
                v = v.rearrange("p (a b) -> p a b", a=dims[0])
            if len(dims) == 3:
                v = v.rearrange("p (a b c) -> p a b c", a=dims[0], b=dims[1])
            if len(dims) == 4:
                v = v.rearrange("p (a b c d) -> p a b c d", a=dims[0], b=dims[1], c=dims[2])
            return v

        ident = s("ident")
        AB = view(0, 2, GP, STEP, GC)
        T1, T2 = view(4096, 8, 9, GC), view(4096 + 1152, 8, 9, GC)
        CA = view(6400, 2, GP, 9, GC)
        Wm = view(11008, 2, GP, 128)
        Tm = view(15104, G, 128)
        u_tok = view(19200, G, STEP, GC)
        y_tok = view(19200, STEP, G, GC)
        Kt = view(19200, G, STEP, GC)
        uT = view(23296, 4, TOK)
        U = view(25600, G, CH)
        H = view(27904, 2, GP, CH + 1)
        Wst = view(0, 2, GP, CH)
        eye_d, st1, st2 = view(5376, G, GC), view(5888, 2, GP, NSEQ), view(6144, 2, GP, NSEQ)
        early = hgT[:, :, :].rearrange("p a b -> p (a b)")
        zt = [early[:, 0:768]] + [view(a, 768) for a in (30240, 23936, 24704, 25472)]
        qs = early[:, 768:1024].rearrange("p (b n) -> p b n", b=NSEQ)
        qTg = [early[:, 1024:1536].rearrange("p (h n) -> p h n", h=4), view(26240, 4, 384)]
        oTg = [view(4352, 4, 192), view(26240, 4, 384)]
        kT, rt = view(31008, TOK), view(31584, 4, 10, 8)
        Pg, Psm = [view(2304, 4, 2 * WIN), view(27776, 4, 2 * WIN)], view(2304, 4, WIN + 64)
        PTg = [view(3328, 2, 4, 128), view(28800, 2, 4, 128)]
        kc, vc = view(23296, NSEQ, WIN), view(23296 + 1024, NSEQ, WIN)
        sg = view(11008, 2, 8, 192)
        gateg = [view(2304, 2, 1, 192), view(23936, 2, 3, 384)]
        partg = [view(2688, 2, 192), view(30848, 2, 384)]
        mTg = [view(23296, KT, 192), view(27776, KT, 384)]
        q2Tg = [view(26240, NH, 192), view(23936, NH, 384)]
        ln1, ln2 = view(13312, 2, DM), view(15360, 2, DM)
        x1 = view(8192, 5, DM)
        ring_u = [view(1024 * i, DM) for i in range(GR1)] + [wring[:, i, :] for i in range(6)]
        ring_v = [view(1024 * (GR1 + i), DM) for i in range(GR1)] + [wring[:, 6 + i, :] for i in range(2)] + \
                 [view(27008 + 1024 * i, DM) for i in range(4)]
        diag = view(17408, DR, 128)
        cand = view(18432, TOPK, TOPK)
        eq = view(18432, NH * TOPK // 2, TOPK)
        acc = view(19456, DM)
        scr = view(20480, 256)
        v16, i16f = view(20736, 2, NH, TOPK), view(20992, 2, NH, TOPK)
        top = view(21248, NH, TOPK)
        posf, ef = view(21376, 2, NH * TOPK), view(21632, 2, NH * TOPK)
        gts, gtf = view(21888, 2, 128), view(22144, 64)
        hdot, hact, aact = view(22208, 2, 128), view(22464, 2, 128), view(22720, 2, 128)
        i16 = view(22976, 2, NH, TOPK).bitcast(U32)
        pos = view(23232, NH, TOPK).bitcast(U32)
        pos2 = view(23360, 2, NH * TOPK).bitcast(U32)
        idx, idxf = view(23616, 2, 128).bitcast(U32), view(23872, 64).bitcast(U32)

        bank = [ctx.enter_context(nc.psum_tensor(f"bank{i}", [128, 512], F32)) for i in range(8)]

        filled = sem("bank_filled")
        drained = {"D": sem("bank_drained_by_vector"), "A": sem("bank_drained_by_scalar"), "S": sem("scores_read_by_vector")}
        w_here = [sem(f"weights_in_slot{i}") for i in range(RING)]
        small_in, xT_in, caches_in, x_in, ln_in = (sem(n) for n in ("small_in", "xT_in", "caches_in", "x_in", "ln_in"))
        xT2_in, x2_in, ln2_in = sem("xT2_in"), sem("x2_in"), sem("ln2_in")
        vstep, astep = sem("vector_step"), sem("scalar_step")
        tables_ready = sem("ssm_tables_ready")
        toep_zero = sem("toeplitz_zeroed")
        kernel_ready = sem("impulse_response_ready")
        toep_in = sem("toeplitz_placed")
        states_ready = sem("chunk_states_ready")
        roped = sem("rotary_done")
        scored = sem("scores_masked")
        expd_s = sem("exponentials_ready")
        probs = sem("probabilities_ready")
        sig = sem("gates_ready")
        merged = sem("merged_part_ready")
        var_s, std_s = sem("variance_ready"), sem("deviation_ready")
        x1_s = sem("x1_tile_ready")
        sc_s, sce_s = sem("top_scores_ready"), sem("top_exponentials_ready")
        idx_s = sem("expert_indices_ready")
        fold_in = sem("folded_sample_in")
        g_u = [sem(f"u_rows_in{i}") for i in range(GR2)]
        g_v = [sem(f"v_rows_in{i}") for i in range(GR2)]
        dots, v_used, v_used_d = sem("u_dot_done"), sem("v_rows_used"), sem("v_rows_used_by_vector")
        act_s, a_s, diag_s = sem("gelu_ready"), sem("activation_ready"), sem("diagonal_ready")
        y_s, y_out = sem("y_tile_ready"), sem("y_stored")
        kv_out, ssm_out, win_out = sem("kv_stored"), sem("ssm_stored"), sem("cached_window_stored")

        block = ctx.enter_context(nc.Block())

        def wait_item(eng, item):
            f, d, a, sc = plan.passed[item]
            eng.wait_ge(filled, f)
            eng.wait_ge(drained["D"], d)
            eng.wait_ge(drained["A"], a)
            if sc:
                eng.wait_ge(drained["S"], sc)

        def group(t):
            return int(t > 1)

        def rel(t):
            return TILES[t][0] - GC0[group(t)][0]

        slot_base, place, nth, before, by_pe, by_dve, on_dve = {}, [], [], [], [], [], []
        for t in ORDER:
            slot_base[t] = len(place)
            share = V_SHARE.get(t, [0] * (n_slots(t) // 8))
            for k in range(n_slots(t)):
                q = len(place)
                place.append(q % GR1 if t < 2 else (q - slot_base[2]) % GR2)
                earlier = [i for i in range(max(0, q - 2 * GR2), q) if place[i] == place[q]]
                before.append(earlier[-1] if earlier else None)
                nth.append(nth[earlier[-1]] + 1 if earlier else 1)
                on_dve.append((k % 8 + 1) * share[k // 8] // 8 > k % 8 * share[k // 8] // 8)
                by_dve.append(sum(on_dve))
                by_pe.append(q + 1 - by_dve[q] + min(len(slot_base) - 1, 2))

        def wait_v_used(eng, q):
            eng.wait_ge(v_used_d if on_dve[q] else v_used, by_dve[q] if on_dve[q] else by_pe[q])

        @block.sync
        def _(sp):
            xv = io["xT"].rearrange("(k p) n -> p k n", p=128)
            sp.dma_start(xT[:, :, 0:192], xv[:, :, 0:192]).then_inc(xT_in, 16)
            for i, p in enumerate(pieces):
                if i == 1:
                    sp.dma_start(xT[:, :, 192:TOK], xv[:, :, 192:TOK]).then_inc(xT2_in, 16)
                if i >= RING:
                    sp.wait_ge(filled, plan.filled[plan.last_use[pieces[i - RING]]])
                if p == (1, "wo", 0):
                    wait_item(sp, ("sc", 0, 1))
                    for t in GROUPS[1]:
                        t0, tn = TILES[t]
                        sp.dma_start(x1[0:tn, t, :], io["x"][t0:t0 + tn, :]).then_inc(x2_in, 16)
                sp.dma_start(wring[:, i % RING, :], io["w"][i]).then_inc(w_here[i % RING], 16)

        @block.gpsimd
        def _(pool):
            nc.gpsimd.memset(Tm[:, :, :], 0.0).then_inc(toep_zero, 1)
            for c, o in (("ckn", "kws"), ("cvn", "vws")):
                pool.dma_start(io[o][:, 0:WIN - STEP, :], io[c][:, STEP:WIN, :]).then_inc(win_out, 16)
            wait_item(pool, ("ut",))
            pool.dma_start(kc, io["kcT"]).then_inc(caches_in, 16)
            pool.dma_start(vc, io["vc"]).then_inc(caches_in, 16)
            pool.wait_ge(toep_zero, 1)
            pool.wait_ge(kernel_ready, 1)
            for i in range(STEP):
                pool.dma_start(Tm[16 * i:16 * i + 16, :, GC * i:128],
                               Kt.rearrange("p g j c -> p g (j c)")[0:16, :, 0:128 - GC * i]).then_inc(toep_in, 16)
            wait_item(pool, ("ht", 1))
            for t in GROUPS[0]:
                t0, tn = TILES[t]
                pool.dma_start(x1[0:tn, t, :], io["x"][t0:t0 + tn, :]).then_inc(x_in, 16)
            pool.dma_start(ln1, io["lnp"].rearrange("p (a b) -> p a b", a=4)[:, 0:2, :]).then_inc(ln_in, 16)
            pool.wait_ge(states_ready, 3)
            pool.dma_start(io["ssm"], fin[:, :, :, :].rearrange("p a b c -> p (a b c)")).then_inc(ssm_out, 16)
            pool.dma_start(ln2, io["lnp"].rearrange("p (a b) -> p a b", a=4)[:, 2:4, :]).then_inc(ln2_in, 16)
            for n, t in enumerate(ORDER):
                ns, base = n_slots(t), slot_base[t]
                pool.wait_ge(idx_s, n + 1)
                if t == 0:
                    pool.wait_ge(fold_in, 16 * 5)
                if t == 2:
                    wait_item(pool, ("wq", 1, 7))
                ind = idxf if t == 0 else idx[:, n % 2, :]

                def u_row(k):
                    q = base + k
                    if before[q] is not None:
                        pool.wait_ge(dots, before[q] + 1)
                    pool.indirect_dma_start(ring_u[place[q]], None, io["pu"],
                                            bass.IndirectOffsetOnAxis(ind[:, k:k + 1], 0)).then_inc(g_u[place[q]], 16)

                def v_row(k):
                    q = base + k
                    if before[q] is not None:
                        wait_v_used(pool, before[q])
                    pool.indirect_dma_start(ring_v[place[q]], None, io["pv"],
                                            bass.IndirectOffsetOnAxis(ind[:, k:k + 1], 0)).then_inc(g_v[place[q]], 16)

                for k in range(ns):
                    u_row(k)
                    if k >= CHK:
                        v_row(k - CHK)
                for k in range(ns - CHK, ns):
                    v_row(k)

        @block.tensor
        def _(pe):
            def enter(key):
                if plan.before[key]:
                    who, n = plan.before[key]
                    pe.wait_ge(drained[who], n)
                return bank[plan.bank[key]]

            def after(key):
                who, n = plan.drained[key]
                pe.wait_ge(drained[who], n)

            def arrived(*p):
                i = piece_no[p]
                pe.wait_ge(w_here[i % RING], 16 * (i // RING + 1))
                return wring[:, i % RING, :]

            mm, tr = nc.tensor.matmul, nc.tensor.transpose

            def do_u():
                for c, (c0, cn) in enumerate(GC0):
                    pe.wait_ge(xT2_in if c else xT_in, 16)
                    for m in range(4):
                        b = enter(("u", c, m))
                        w = arrived(0, "u", m).rearrange("p (k n) -> p k n", k=KT)
                        for k in range(KT):
                            last = mm(b[:, 0:cn], w[:, k, :], xT[:, k, c0:c0 + cn], start=k == 0, stop=k == KT - 1)
                        last.then_inc(filled, 1)

            def do_ut():
                pe.wait_ge(small_in, 16)
                after(("u", 1, 3))
                for i in range(STEP):
                    b = enter(("ut", i))
                    for m in range(4):
                        last = tr(b[0:CH, 128 * m:128 * m + 128], uT[:, m, i::STEP], ident)
                    last.then_inc(filled, 1)

            def do_uc():
                after(("ut", 7))
                for i in range(8):
                    b = enter(("uc", i))
                    for g in range(4):
                        last = tr(b[:, CH * g:CH * g + CH], u_tok[0:CH, 4 * i + g, :, :].rearrange("p s c -> p (s c)"), ident[0:CH, 0:CH])
                    last.then_inc(filled, 1)

            def do_wt():
                pe.wait_ge(tables_ready, 1)
                for ri in range(2):
                    for i in range(4):
                        b = enter(("wt", ri, i))
                        for g in range(4):
                            last = tr(b[:, 128 * g:128 * g + 128], AB[:, ri, 4 * i + g, :, :].rearrange("p s c -> p (s c)"), ident)
                        last.then_inc(filled, 1)

            def do_k():
                for par in range(2):
                    rows = slice(64 * par, 64 * par + 64)
                    for i in range(4):
                        b = enter(("k", par, i))
                        for g in range(4):
                            for ri in range(2):
                                last = mm(b[0:GC, 128 * g:128 * g + 128], Bb[rows, ri, 4 * i + g, :],
                                          CA[rows, ri, 4 * i + g, 0:STEP, :].rearrange("p j c -> p (j c)"), start=ri == 0, stop=ri == 1)
                        last.then_inc(filled, 1)

            def do_ws():
                for j in (2, 3):
                    after(("wt", 1, j))
                after(("uc", 7))
                for ri in range(2):
                    for i in range(4):
                        b = enter(("ws", ri, i))
                        for g in range(4):
                            for par in range(2):
                                last = mm(b[64 * par:64 * par + 64, CH * g:CH * g + CH], Wm[:, ri, 4 * i + g, 64 * par:64 * par + 64],
                                          U[:, 2 * (4 * i + g) + par, :], start=True, stop=True)
                        last.then_inc(filled, 1)

            def do_y(part):
                c0, cn = CHUNKS[part]
                pe.wait_ge(toep_in, 16 * STEP)
                pe.wait_ge(states_ready, part + 1)
                for par in range(2):
                    rows = slice(64 * par, 64 * par + 64)
                    for i in range(4):
                        b = enter(("y", part, par, i))
                        for g in range(4):
                            gp = 4 * i + g
                            o = b[0:cn, 128 * g:128 * g + 128]
                            mm(o, U[:, 2 * gp + par, c0:c0 + cn], Tm[:, 2 * gp + par, :], start=True, stop=False)
                            for ri in range(2):
                                last = mm(o, H[rows, ri, gp, c0:c0 + cn], CA[rows, ri, gp, 1:9, :].rearrange("p j c -> p (j c)"),
                                          start=False, stop=ri == 1)
                        last.then_inc(filled, 1)

            def do_ht(part):
                cn = CHUNKS[part][1]
                after(("y", part, 1, 3))
                for m in range(4):
                    for hf in range(2):
                        b = enter(("ht", part, m, hf))
                        for i in range(4):
                            last = tr(b[:, cn * i:cn * i + cn], y_tok[0:cn, 4 * hf + i, 8 * m:8 * m + 8, :].rearrange("p g c -> p (g c)"),
                                      ident[0:cn, 0:cn])
                        last.then_inc(filled, 1)

            def do_qkv(t):
                t0, tn = TILES[t]
                for what, n in (("q", 512), ("kv", 256)):
                    b = enter((what, t))
                    kp = 1024 // n
                    for k in range(KT):
                        w = arrived(group(t), what, k // kp).rearrange("p (k n) -> p k n", n=n)
                        last = mm(b[0:tn, 0:n], xT[:, k, t0:t0 + tn], w[:, k % kp, :], start=k == 0, stop=k == KT - 1)
                    last.then_inc(filled, 1)

            def do_turn(t):
                tn = TILES[t][1]
                pe.wait_ge(roped, plan.index[("qkv", t)])
                b = enter(("qt", t))
                for i in range(4):
                    last = tr(b[:, 128 * i:128 * i + tn], zt[t][0:tn, 128 * i:128 * i + 128], ident[0:tn, 0:tn])
                last.then_inc(filled, 1)
                b = enter(("kt", t))
                tr(b[:, 0:tn], zt[t][0:tn, 512:640], ident[0:tn, 0:tn]).then_inc(filled, 1)

            def do_ss():
                after(("kt", 0))
                pe.wait_ge(caches_in, 32)
                for kv in range(2):
                    rows = slice(64 * kv, 64 * kv + 64)
                    for hf in range(2):
                        b = enter(("ss", kv, hf))
                        for i in range(4):
                            q = qs[rows, 4 * hf + i, :]
                            mm(b[32 * i:32 * i + 32, 0:WIN], q, kc[rows, 4 * hf + i, :], start=True, stop=True)
                            last = mm(b[32 * i:32 * i + 32, WIN:WIN + 64], q, kT[rows, 0:64], start=True, stop=True)
                        last.then_inc(filled, 1)

            def do_pvs():
                PT = PTg[0]
                pe.wait_ge(probs, 1)
                b = enter(("spc",))
                for i in range(4):
                    last = tr(b[:, 128 * i:128 * i + 128], Psm[:, i, 0:WIN], ident)
                last.then_inc(filled, 1)
                b = enter(("spn",))
                for i in range(4):
                    last = tr(b[0:64, 128 * i:128 * i + 128], Psm[:, i, WIN:WIN + 64], ident)
                last.then_inc(filled, 1)
                b = enter(("so",))
                after(("spn",))
                for kv in range(2):
                    for i in range(NSEQ):
                        o = b[64 * kv:64 * kv + 64, 32 * i:32 * i + 32]
                        cols = slice(32 * (i % 4), 32 * (i % 4) + 32)
                        mm(o, vc[:, i, 64 * kv:64 * kv + 64], PT[:, 0, 2 * kv + i // 4, cols], start=True, stop=False)
                        last = mm(o, zt[0][0:64, 640 + 64 * kv:704 + 64 * kv], PT[0:64, 1, 2 * kv + i // 4, cols], start=False, stop=True)
                last.then_inc(filled, 1)

            def do_s(j, kv):
                t = j + 1
                t0, k0, off = TILES[t][0], TILES[t][0] - (128 if j else 0), 0 if j else 128
                after(("kt", 4 if j else 1))
                rows = slice(64 * kv, 64 * kv + 64)
                for hf in range(2):
                    b = enter(("s", j, kv, hf))
                    for i in range(2):
                        last = mm(b[:, 256 * i + off:256 * i + 256], qTg[group(t)][rows, 2 * hf + i, rel(t) - (0 if j else 64):][:, 0:128],
                                  kT[rows, k0:t0 + 128], start=True, stop=True)
                    last.then_inc(filled, 1)

            def do_pv(j, kv):
                P, PT = Pg[group(j + 1)], PTg[group(j + 1)]
                pe.wait_ge(probs, 1 + plan.index[("s", j, kv)])
                for i in range(2):
                    b = enter(("pt", j, kv, i))
                    for e in range(4):
                        last = tr(b[:, 128 * e:128 * e + 128], P[:, 2 * i + e // 2, 128 * (e % 2):128 * (e % 2) + 128], ident)
                    last.then_inc(filled, 1)
                b = enter(("o", j, kv))
                after(("pt", j, kv, 1))
                for hp in range(4):
                    o = b[64 * kv:64 * kv + 64, 128 * hp:128 * hp + 128]
                    for hf in range(0 if j else 1, 2):
                        last = mm(o, zt[j + hf][:, 640 + 64 * kv:704 + 64 * kv],
                                  PT[:, hp // 2, 2 * (hp % 2) + hf, :], start=hf == (0 if j else 1), stop=hf == 1)
                last.then_inc(filled, 1)

            def rows_of(what, g, m):
                c0, cn = GC0[g]
                src, k0, kn = {"gs": (xT, 0, 8), "ga": (xT, 0, 8), "gb": (hgT, 4, 4), "gl": (hgT, 0, 4), "up": (oTg[g], 4 * (m % 2), 4)}[what]
                s0 = 0 if what == "up" else c0
                b = enter((what, g, m))
                w = (arrived(g, "up", m // 2) if what == "up" else arrived(g, "glu", m) if what in ("gb", "gl")
                     else arrived(g, what, m)).rearrange("p (k n) -> p k n", k=8)
                for k in range(kn):
                    last = mm(b[:, 0:cn], w[:, k0 + k, :], src[:, k, s0:s0 + cn], start=k == 0, stop=k == kn - 1)
                last.then_inc(filled, 1)

            def do_gates(m):
                rows_of("gs", 0, m)
                rows_of("ga", 0, m)

            def do_merge(g, m):
                if m == 0:
                    after(("o", 3 if g else 0, 1))
                    after(("ht", g, 3, 1))
                for what in (("gs", "ga") if g else ()) + ("gb", "gl", "up"):
                    rows_of(what, g, m)

            def do_wo(t):
                g, tn = group(t), TILES[t][1]
                after(("up", g, 7))
                for hf in range(2):
                    b = enter(("wo", t, hf))
                    for k in range(KT):
                        w = arrived(g, "wo", k)
                        last = mm(b[0:tn, :], mTg[g][:, k, rel(t):rel(t) + tn], w[:, 512 * hf:512 * hf + 512], start=k == 0, stop=k == KT - 1)
                    last.then_inc(filled, 1)

            def do_xt(t):
                tn = TILES[t][1]
                pe.wait_ge(x1_s, plan.index[("wo", t)])
                for hf in range(2):
                    b = enter(("xt", t, hf))
                    for i in range(4):
                        k = 4 * hf + i
                        last = tr(b[:, 128 * i:128 * i + tn], x1[0:tn, t, 128 * k:128 * k + 128], ident[0:tn, 0:tn])
                    last.then_inc(filled, 1)

            def do_wq(g, h):
                c0, cn = GC0[g]
                after(("xt", GROUPS[g][-1], 1))
                b = enter(("wq", g, h))
                w = arrived(g, "wq", h).rearrange("p (k n) -> p k n", k=8)
                for k in range(KT):
                    last = mm(b[:, 0:cn], w[:, k, :], xT[:, k, c0:c0 + cn], start=k == 0, stop=k == KT - 1)
                last.then_inc(filled, 1)

            def do_sc(t, i):
                g, tn = group(t), TILES[t][1]
                after(("wq", g, 6))
                after(("wq", g, 7))
                k12 = s("k12", NH, KEYS)
                for side in range(2):
                    rows = slice(64 * side, 64 * side + 64)
                    b = enter(("sc", t, side, i))
                    for h in range(4):
                        last = mm(b[0:tn, 128 * h:128 * h + 128], q2Tg[g][rows, 4 * i + h, rel(t):rel(t) + tn], k12[rows, 4 * i + h, :],
                                  start=True, stop=True)
                    last.then_inc(filled, 1)

            def weigh(t, c):
                tn, ns, base = TILES[t][1], n_slots(t), slot_base[t]
                for k in range(CHK * c, CHK * c + CHK):
                    q = base + k
                    if k == 0:
                        enter(("po", t, 0)), enter(("po", t, 1))
                    if on_dve[q]:
                        continue
                    d = q - by_dve[q]
                    pe.wait_ge(diag_s, d + 1)
                    pe.wait_ge(g_v[place[q]], 16 * nth[q])
                    for hf in range(2):
                        last = mm(bank[6 + hf][0:tn, :], diag[:, d % DR, 0:tn], ring_v[place[q]][:, 512 * hf:512 * hf + 512],
                                  start=k == 0, stop=t not in V_SHARE and k == ns - 1)
                    last.then_inc(v_used, 1)
                if c == ns // CHK - 1 and t < 2:
                    pe.wait_ge(v_used_d, by_dve[base + ns - 1])
                    for hf in range(2):
                        last = mm(bank[6 + hf][0:tn, :], s("fold") if t == 0 else ident, acc[:, 512 * hf:512 * hf + 512],
                                  start=False, stop=True)
                    last.then_inc(v_used, 1)

            def do_peer(t, c):
                if c:
                    weigh(t, c - 1)

            def do_last(t):
                weigh(t, n_slots(t) // CHK - 1)

            here = {"u": do_u, "ut": do_ut, "uc": do_uc, "wt": do_wt, "k": do_k, "ws": do_ws, "y": do_y, "ht": do_ht, "qkv": do_qkv,
                    "turn": do_turn, "ss": do_ss, "pvs": do_pvs, "s": do_s, "pv": do_pv, "gates": do_gates, "merge": do_merge,
                    "wo": do_wo, "xt": do_xt, "wq": do_wq, "sc": do_sc, "peer": do_peer, "last": do_last}
            for item in mixer_first(plan.items):
                if item[0] in here:
                    here[item[0]](*item[1:])

        @block.vector
        def _(dve):
            V = nc.vector
            steps = [0]

            def step(ins):
                steps[0] += 1
                ins.then_inc(vstep, 1)
                dve.wait_ge(vstep, steps[0])

            def drain(key, ins):
                who, n = plan.drained[key]
                ins.then_inc(drained[who], 1)
                dve.wait_ge(drained[who], n)

            def full(key):
                dve.wait_ge(filled, plan.filled[key])
                return bank[plan.bank[key]]

            def cmul(out, x, y, t1, t2):
                n = x.shape[2]
                step(V.tensor_tensor(t1, x, y[:, 0:1, :].broadcast_to([128, 2, n]), ALU.mult))
                step(V.tensor_tensor(t2, x[:, 1::-1, :], y[:, 1:2, :].broadcast_to([128, 2, n]), ALU.mult))
                step(V.tensor_tensor(out[:, 0, :], t1[:, 0, :], t2[:, 0, :], ALU.subtract))
                step(V.tensor_tensor(out[:, 1, :], t1[:, 1, :], t2[:, 1, :], ALU.add))

            ta, tb, w, wk, T, E = (cx[:, i, :, :] for i in range(6))
            a_, num = cx[:, 6, :, :], cx[:, 8, :, :]

            def do_tables():
                dve.wait_ge(small_in, 16)
                dve.wait_ge(astep, 1)
                step(V.tensor_copy(a_[:, 0, :], s("are")))
                step(V.tensor_copy(a_[:, 1, :], s("aim")))
                step(V.scalar_tensor_tensor(out=w, in0=a_, scalar=1.0 / 256, in1=cx[:, 7, 0:1, :].broadcast_to([128, 2, GP]),
                                            op0=ALU.mult, op1=ALU.mult))
                step(V.tensor_scalar(T, w, 1.0 / 8, None, ALU.mult))
                step(V.tensor_scalar(T[:, 0, :], T[:, 0, :], 1.0, None, ALU.add))
                for k in range(7, 0, -1):
                    step(V.tensor_scalar(wk, w, 1.0 / k, None, ALU.mult))
                    cmul(T, wk, T, ta, tb)
                    if k > 1:
                        step(V.tensor_scalar(T[:, 0, :], T[:, 0, :], 1.0, None, ALU.add))
                step(V.tensor_copy(E, T))
                for _ in range(8):
                    step(V.tensor_copy(wk, E))
                    step(V.tensor_scalar(wk[:, 0, :], wk[:, 0, :], 2.0, None, ALU.add))
                    cmul(E, wk, E, ta, tb)
                step(V.tensor_tensor(ta, a_, a_, ALU.mult))
                step(V.tensor_tensor(tb[:, 0, :], ta[:, 0, :], ta[:, 1, :], ALU.add))
                step(V.reciprocal(tb[:, 1, :], tb[:, 0, :]))
                step(V.tensor_tensor(wk, a_, tb[:, 1:2, :].broadcast_to([128, 2, GP]), ALU.mult))
                step(V.tensor_scalar(wk[:, 1, :], wk[:, 1, :], -1.0, None, ALU.mult))
                cmul(num, E, wk, ta, tb)
                bb, cc = s("bb", 2, GP * GC).rearrange("p a (g c) -> p a g c", c=GC), s("cc", 2, GP * GC).rearrange("p a (g c) -> p a g c", c=GC)
                small1 = T1.rearrange("p a b c -> p (a b c)")[:, 0:256].rearrange("p (g c) -> p g c", c=GC)
                small2 = T2.rearrange("p a b c -> p (a b c)")[:, 0:256].rearrange("p (g c) -> p g c", c=GC)

                def over_c(x):
                    return x.unsqueeze(2).broadcast_to([128, GP, GC])

                step(V.tensor_tensor(small1, bb[:, 0], over_c(num[:, 0, :]), ALU.mult))
                step(V.tensor_tensor(small2, bb[:, 1], over_c(num[:, 1, :]), ALU.mult))
                step(V.tensor_tensor(Bb[:, 0], small1, small2, ALU.subtract))
                step(V.tensor_tensor(small1, bb[:, 0], over_c(num[:, 1, :]), ALU.mult))
                step(V.tensor_tensor(small2, bb[:, 1], over_c(num[:, 0, :]), ALU.mult))
                step(V.tensor_tensor(Bb[:, 1], small1, small2, ALU.add))
                step(V.memset(pw[:, 0, :, 0], 1.0))
                step(V.memset(pw[:, 1, :, 0], 0.0))
                step(V.tensor_scalar(pw[:, 0, :, 1], E[:, 0, :], 1.0, None, ALU.add))
                step(V.tensor_copy(pw[:, 1, :, 1], E[:, 1, :]))
                for j in range(2, 9):
                    cmul(pw[:, :, :, j], pw[:, :, :, j - 1], pw[:, :, :, 1], ta, tb)
                step(V.tensor_copy(a8[:, 0], pw[:, 0:1, :, 8].broadcast_to([128, 2, GP])))
                step(V.tensor_scalar(a8[:, 1, 0, :], pw[:, 1, :, 8], -1.0, None, ALU.mult))
                step(V.tensor_copy(a8[:, 1, 1, :], pw[:, 1, :, 8]))


                def outer(out0, out1, x, powers, hf, n, sign):
                    g = slice(8 * hf, 8 * hf + 8)
                    t1, t2 = T1[:, :, 0:n, :], T2[:, :, 0:n, :]
                    X = [x[:, r, g, :].unsqueeze(2).broadcast_to([128, 8, n, GC]) for r in range(2)]
                    Q = [powers[r][:, g, :].unsqueeze(3).broadcast_to([128, 8, n, GC]) for r in range(2)]
                    step(V.tensor_tensor(t1, X[0], Q[0], ALU.mult))
                    step(V.tensor_tensor(t2, X[1], Q[1], ALU.mult))
                    step(V.tensor_tensor(out0[:, g], t1, t2, ALU.subtract))
                    step(V.tensor_tensor(t1, X[0], Q[1], ALU.mult))
                    step(V.tensor_tensor(t2, X[1], Q[0], ALU.mult))
                    if sign > 0:
                        step(V.tensor_tensor(out1[:, g], t1, t2, ALU.add))
                    else:
                        step(V.tensor_tensor(t1, t1, t2, ALU.add))
                        step(V.tensor_scalar(out1[:, g], t1, -1.0, None, ALU.mult))

                for hf in range(2):
                    outer(CA[:, 0], CA[:, 1], cc, [pw[:, r, :, :] for r in range(2)], hf, 9, -1)
                for hf in range(2):
                    outer(AB[:, 0], AB[:, 1], Bb, [pw[:, r, :, 7::-1] for r in range(2)], hf, 8, 1)
                step(V.tensor_copy(H[:, :, :, 0:NSEQ], s("h0", 2, GP, NSEQ)))
                V.memset(H[:, :, :, NSEQ:NSEQ + 1], 0.0).then_inc(tables_ready, 1)
                dve.wait_ge(tables_ready, 1)

            def do_wt():
                for ri in range(2):
                    for i in (1, 3):
                        b = full(("wt", ri, i))
                        drain(("wt", ri, i), V.tensor_copy(Wm[:, ri, 4 * i:4 * i + 4, :].rearrange("p g n -> p (g n)"), b[:, :]))

            def do_k():
                wait_item(dve, ("uc",))
                for par in range(2):
                    for i in (1, 3):
                        b = full(("k", par, i))
                        drain(("k", par, i), V.tensor_copy(Kt[0:GC, 8 * i + par:8 * i + par + 7:2, :, :].rearrange("p g j c -> p g (j c)"),
                                                           b[0:GC, :].rearrange("p (g n) -> p g n", g=4)))
                dve.wait_ge(drained["A"], plan.drained[("k", 1, 2)][1])
                step(V.tensor_tensor(eye_d[0:GC], s("dskip", G, GC)[0:GC], ident[0:GC, 0:GC].unsqueeze(1).broadcast_to([GC, G, GC]), ALU.mult))
                V.tensor_tensor(Kt[0:GC, :, 0, :], Kt[0:GC, :, 0, :], eye_d[0:GC], ALU.add).then_inc(kernel_ready, 1)

            def do_ws():
                for ri in range(2):
                    for i in (1, 3):
                        b = full(("ws", ri, i))
                        drain(("ws", ri, i), V.tensor_copy(Wst[:, ri, 4 * i:4 * i + 4, :].rearrange("p g n -> p (g n)"), b[:, 0:4 * CH]))

            def do_rec(part):
                dve.wait_ge(drained["A"], plan.drained[("ws", 1, 2)][1])
                c0, cn = CHUNKS[part]
                for c in range(max(c0, NSEQ), c0 + cn):
                    step(V.tensor_tensor(ta, H[:, :, :, c], a8[:, 0], ALU.mult))
                    step(V.tensor_tensor(tb, H[:, 1::-1, :, c], a8[:, 1], ALU.mult))
                    step(V.tensor_tensor(ta, ta, Wst[:, :, :, c], ALU.add))
                    ins = V.tensor_tensor(H[:, :, :, c + 1], ta, tb, ALU.add)
                    if c < c0 + cn - 1:
                        step(ins)
                    else:
                        ins.then_inc(states_ready, 1)
                        dve.wait_ge(states_ready, part + 1)
                if part:
                    step(V.tensor_copy(fin[:, :, :, 0], H[:, :, :, CH]))
                    step(V.tensor_tensor(st1, H[:, :, :, 0:NSEQ], a8[:, 0].unsqueeze(3).broadcast_to([128, 2, GP, NSEQ]), ALU.mult))
                    step(V.tensor_tensor(st2, H[:, 1::-1, :, 0:NSEQ], a8[:, 1].unsqueeze(3).broadcast_to([128, 2, GP, NSEQ]), ALU.mult))
                    step(V.tensor_tensor(st1, st1, st2, ALU.add))
                    V.tensor_tensor(fin[:, :, :, 1:1 + NSEQ], st1, Wst[:, :, :, 0:NSEQ], ALU.add).then_inc(states_ready, 1)

            rope = s("rope", 5, 2, 8)

            def do_qkv(t):
                tn, z = TILES[t][1], zt[t]
                if t == 2:
                    wait_item(dve, ("ht", 1))
                b = full(("q", t))
                drain(("q", t), V.tensor_tensor(z[0:tn, 0:512], b[0:tn, :], s("bqkv")[0:tn, 0:512], ALU.add))
                b = full(("kv", t))
                drain(("kv", t), V.tensor_tensor(z[0:tn, 512:768], b[0:tn, 0:256], s("bqkv")[0:tn, 512:768], ALU.add))
                hd = z[0:tn, 0:640].rearrange("p (h d) -> p h d", d=HD)
                lo, hi = hd[:, :, 0:8], hd[:, :, 8:16]
                cos, sin = (rope[0:tn, t, r, :].unsqueeze(1).broadcast_to([tn, 10, 8]) for r in range(2))
                step(V.tensor_tensor(rt[0:tn, 0], lo, cos, ALU.mult))
                step(V.tensor_tensor(rt[0:tn, 1], hi, sin, ALU.mult))
                step(V.tensor_tensor(rt[0:tn, 2], hi, cos, ALU.mult))
                step(V.tensor_tensor(rt[0:tn, 3], lo, sin, ALU.mult))
                step(V.tensor_tensor(lo, rt[0:tn, 0], rt[0:tn, 1], ALU.subtract))
                V.tensor_tensor(hi, rt[0:tn, 2], rt[0:tn, 3], ALU.add).then_inc(roped, 1)
                dve.wait_ge(roped, plan.index[("qkv", t)])

            def softmax(n, scores, sink, width, st):
                mx, ex, sm, rs = (stat[:, 8 * i:8 * i + width] for i in range(4))
                step(V.tensor_reduce(mx, scores, AX, ALU.max))
                step(V.tensor_tensor(mx, mx, sink, ALU.max))
                step(V.tensor_tensor(ex, sink, mx, ALU.subtract))
                V.tensor_tensor(scores, scores, mx.unsqueeze(2).broadcast_to([128, width, st]), ALU.subtract).then_inc(scored, 1)
                dve.wait_ge(expd_s, n)
                step(V.tensor_reduce(sm, scores, AX, ALU.add))
                step(V.tensor_tensor(sm, sm, ex, ALU.add))
                step(V.reciprocal(rs, sm))
                V.tensor_tensor(scores, scores, rs.unsqueeze(2).broadcast_to([128, width, st]), ALU.mult).then_inc(probs, 1)
                dve.wait_ge(probs, n)

            masks, maskp = s("masks", 2, WIN + 64), s("maskp")

            def do_ss():
                for kv in range(2):
                    for hf in range(2):
                        b = full(("ss", kv, hf))
                        drain(("ss", kv, hf), V.scalar_tensor_tensor(out=Psm[:, 2 * kv + hf, :], in0=b[:, 0:WIN + 64], scalar=HD ** -0.5,
                                                                     in1=masks[:, hf, :], op0=ALU.mult, op1=ALU.add))
                sk = stat[:, 60:64]
                step(V.tensor_copy(sk.rearrange("p (a b) -> p a b", a=2), s("sinks").unsqueeze(2).broadcast_to([128, 2, 2])))
                softmax(1, Psm, sk, 4, WIN + 64)

            def do_pvs():
                b = full(("so",))
                for kv in range(2):
                    rows = slice(64 * kv, 64 * kv + 64)
                    ins = V.tensor_copy(oTg[0][rows, :, 0:64].rearrange("p h (b q) -> p b h q", q=8),
                                        b[rows, 0:256].rearrange("p (b h q) -> p b h q", b=8, h=4))
                    step(ins) if kv == 0 else drain(("so",), ins)

            def do_s(j, kv):
                n, P = plan.index[("s", j, kv)], Pg[group(j + 1)]
                for hf in range(2):
                    b = full(("s", j, kv, hf))
                    if hf == 0:
                        prev = plan.items[:plan.items.index(("s", j, kv))]
                        dve.wait_ge(filled, max(plan.filled[k] for k in (("spn",), *[("pt", *i[1:], 1) for i in prev if i[0] == "pv"])))
                    o = P[:, 2 * hf:2 * hf + 2, :]
                    if j == 0:
                        step(V.memset(o[:, :, 0:128], NEG))
                        drain(("s", j, kv, hf), V.scalar_tensor_tensor(
                            out=o[:, :, 128:256], in0=b[:, :].rearrange("p (a n) -> p a n", a=2)[:, :, 128:256], scalar=HD ** -0.5,
                            in1=maskp[:, 128:256].unsqueeze(1).broadcast_to([128, 2, 128]), op0=ALU.mult, op1=ALU.add))
                    else:
                        drain(("s", j, kv, hf), V.scalar_tensor_tensor(
                            out=o, in0=b[:, :].rearrange("p (a n) -> p a n", a=2), scalar=HD ** -0.5,
                            in1=maskp.unsqueeze(1).broadcast_to([128, 2, 256]), op0=ALU.mult, op1=ALU.add))
                softmax(1 + n, P, s("sinkp")[:, 4 * kv:4 * kv + 4], 4, 2 * WIN)

            def do_pv(j, kv):
                t = j + 1
                c, rows = rel(t), slice(64 * kv, 64 * kv + 64)
                b = full(("o", j, kv))
                drain(("o", j, kv), V.tensor_copy(oTg[group(t)][rows, :, c:c + 128], b[rows, :].rearrange("p (h n) -> p h n", h=4)))

            def do_merge(g, m):
                n, cn = 8 * g + m, GC0[g][1]
                if g and m == 0:
                    wait_item(dve, ("pv", 3, 1))
                    dve.wait_ge(kv_out, 64)
                gt, q = gateg[g][:, n % 2, :, :], partg[g]
                s_gate, a_gate = (gt[:, 0], gt[:, 1]) if g else (sg[:, 0, m], sg[:, 1, m])
                b = full(("gl", g, m))
                dve.wait_ge(drained["A"], plan.drained[("gb", g, m)][1])
                drain(("gl", g, m), V.scalar_tensor_tensor(out=q[:, 0], in0=b[:, 0:cn], scalar=s("bglu")[:, m:m + 1], in1=gt[:, 2 if g else 0],
                                                           op0=ALU.add, op1=ALU.mult))
                step(V.tensor_tensor(q[:, 0], q[:, 0], s_gate, ALU.mult))
                b = full(("up", g, m))
                step(V.tensor_tensor(q[:, 1], b[:, 0:cn], a_gate, ALU.mult))
                drain(("up", g, m), V.tensor_tensor(mTg[g][:, m, :], q[:, 0], q[:, 1], ALU.add))

            norms = [0]

            def layer_norm(out, r, tn, ln):
                norms[0] += 1
                st, mv = stat[0:tn, 64:76], stat[0:tn, 76:78]
                for hf in range(2):
                    step(V.bn_stats(st[:, 6 * hf:6 * hf + 6], r[:, 512 * hf:512 * hf + 512]))
                step(V.bn_aggr(mv, st))
                V.tensor_scalar(stat[0:tn, 78:79], mv[:, 1:2], EPS, None, ALU.add).then_inc(var_s, 1)
                dve.wait_ge(std_s, norms[0])
                step(V.reciprocal(stat[0:tn, 78:79], stat[0:tn, 79:80]))
                step(V.tensor_scalar(r, r, mv[:, 0:1], stat[0:tn, 78:79], ALU.subtract, ALU.mult))
                step(V.tensor_tensor(r, r, ln[0:tn, 0, :], ALU.mult))
                return V.tensor_tensor(out, r, ln[0:tn, 1, :], ALU.add)

            def do_wo(t):
                tn = TILES[t][1]
                dve.wait_ge(x2_in if t > 1 else x_in, 16 * len(GROUPS[group(t)]))
                dve.wait_ge(ln_in, 16)
                for hf in range(2):
                    b = full(("wo", t, hf))
                    half = slice(512 * hf, 512 * hf + 512)
                    drain(("wo", t, hf), V.scalar_tensor_tensor(out=x1[0:tn, t, half], in0=x1[0:tn, t, half], scalar=ALPHA,
                                                                in1=b[0:tn, :], op0=ALU.mult, op1=ALU.add))
                layer_norm(x1[0:tn, t, :], x1[0:tn, t, :], tn, ln1).then_inc(x1_s, 1)
                dve.wait_ge(x1_s, plan.index[("wo", t)])

            def do_wq(g, h):
                if h % 2:
                    b = full(("wq", g, h))
                    drain(("wq", g, h), V.tensor_copy(q2Tg[g][:, h, :], b[:, 0:GC0[g][1]]))

            def top_keys(t, h):
                tn = TILES[t][1]
                for side in range(2):
                    b = full(("sc", t, side, h // 4))
                    sc = b[0:tn, 128 * (h % 4):128 * (h % 4) + 128]
                    va, vb = v16[0:tn, side, h, 0:8], v16[0:tn, side, h, 8:16]
                    ia, ib = i16[0:tn, side, h, 0:8], i16[0:tn, side, h, 8:16]
                    rest = scr[0:tn, 0:128]
                    step(V.max(out=va, in_=sc))
                    step(V.max_index(out=ia, in_max=va, in_values=sc))
                    ins = V.match_replace(out=rest, in_to_replace=va, in_values=sc, imm_value=-3.0e38)
                    drain(("sc", t, side, h // 4), ins) if h % 4 == 3 else step(ins)
                    step(V.max(out=vb, in_=rest))
                    step(V.max_index(out=ib, in_max=vb, in_values=rest))
                cd = cand[0:tn].rearrange("p a b -> p (a b)")
                step(V.tensor_tensor(cand[0:tn], v16[0:tn, 0, h, :].unsqueeze(2).broadcast_to([tn, TOPK, TOPK]),
                                     v16[0:tn, 1, h, :].unsqueeze(1).broadcast_to([tn, TOPK, TOPK]), ALU.add))
                rest = scr[0:tn, 0:256]
                step(V.max(out=top[0:tn, h, 0:8], in_=cd))
                step(V.max_index(out=pos[0:tn, h, 0:8], in_max=top[0:tn, h, 0:8], in_values=cd))
                step(V.match_replace(out=rest, in_to_replace=top[0:tn, h, 0:8], in_values=cd, imm_value=-3.0e38))
                step(V.max(out=top[0:tn, h, 8:16], in_=rest))
                step(V.max_index(out=pos[0:tn, h, 8:16], in_max=top[0:tn, h, 8:16], in_values=rest))

            def do_choose(t, part):
                n, tn = ORDER.index(t), TILES[t][1]
                gt = gts[0:tn, n % 2, :].rearrange("p (h k) -> p h k", h=NH)
                if part == 0:
                    V.tensor_tensor(gt, top[0:tn], top[0:tn, :, 0:1].broadcast_to([tn, NH, TOPK]), ALU.subtract).then_inc(sc_s, 1)
                    step(V.tensor_scalar(pos2[0:tn, 0, :], pos[0:tn].rearrange("p h k -> p (h k)"), 4, None, ALU.logical_shift_right))
                    step(V.tensor_scalar(pos2[0:tn, 1, :], pos[0:tn].rearrange("p h k -> p (h k)"), 15, None, ALU.bitwise_and))
                    step(V.tensor_copy(posf[0:tn], pos2[0:tn]))
                    step(V.tensor_copy(i16f[0:tn], i16[0:tn]))
                if part < 2:
                    for side in range(2):
                        half = slice(64 * part, 64 * part + 64)
                        heads = eq[0:tn].rearrange("p (h k) a -> p h k a", h=NH // 2)
                        step(V.tensor_tensor(eq[0:tn], posf[0:tn, side, half].unsqueeze(2).broadcast_to([tn, 64, TOPK]),
                                             s("iota")[0:tn].unsqueeze(1).broadcast_to([tn, 64, TOPK]), ALU.is_equal))
                        step(V.tensor_tensor(heads, heads, i16f[0:tn, side, 4 * part:4 * part + 4].unsqueeze(2).broadcast_to(
                                             [tn, NH // 2, TOPK, TOPK]), ALU.mult))
                        step(V.tensor_reduce(ef[0:tn, side, half], eq[0:tn], AX, ALU.add))
                    return
                step(V.scalar_tensor_tensor(out=ef[0:tn, 0, :], in0=ef[0:tn, 0, :], scalar=float(KEYS), in1=ef[0:tn, 1, :],
                                            op0=ALU.mult, op1=ALU.add))
                step(V.tensor_copy(idx[0:tn, n % 2, :], ef[0:tn, 0, :]))
                dve.wait_ge(sce_s, n + 1)
                sm, rs = stat[0:tn, 20:28], stat[0:tn, 28:36]
                step(V.tensor_reduce(sm, gt, AX, ALU.add))
                step(V.reciprocal(rs, sm))
                V.tensor_tensor(gt, gt, rs.unsqueeze(2).broadcast_to([tn, NH, TOPK]), ALU.mult).then_inc(idx_s, 1)
                dve.wait_ge(idx_s, n + 1)

            def do_top(t, h):
                if (t, h) == (ORDER[0], 0):
                    wait_item(dve, ("ht", 1))
                top_keys(t, h)

            done = [0]

            def gated(t, c):
                n = ORDER.index(t)
                gt = gtf if t == 0 else gts[:, n % 2, :]
                done[0] += 1
                dve.wait_ge(act_s, done[0])
                k = slice(CHK * c, CHK * c + CHK)
                V.tensor_tensor(aact[:, n % 2, k], hact[:, n % 2, k], gt[:, k], ALU.mult).then_inc(a_s, 1)

            def add_row(t, k):
                n, q = ORDER.index(t), slot_base[t] + k
                if not on_dve[q]:
                    return
                dve.wait_ge(a_s, done[0])
                dve.wait_ge(g_v[place[q]], 16 * nth[q])
                if not any(on_dve[slot_base[t]:q]):
                    if n:
                        dve.wait_ge(v_used, by_pe[slot_base[t] - 1] + 1)
                    V.tensor_scalar(acc, ring_v[place[q]], aact[:, n % 2, k:k + 1], None, ALU.mult).then_inc(v_used_d, 1)
                else:
                    dve.wait_ge(v_used_d, by_dve[q] - 1)
                    V.scalar_tensor_tensor(out=acc, in0=ring_v[place[q]], scalar=aact[:, n % 2, k:k + 1], in1=acc,
                                           op0=ALU.mult, op1=ALU.add).then_inc(v_used_d, 1)

            def do_peer(t, c):
                n, base = ORDER.index(t), slot_base[t]
                if t == 0 and c == 0:
                    dve.wait_ge(fold_in, 16 * 5)
                for k in range(CHK * c, CHK * c + CHK):
                    q = base + k
                    dve.wait_ge(g_u[place[q]], 16 * nth[q])
                    V.tensor_tensor_reduce(out=ring_u[place[q]], in0=ring_u[place[q]], in1=x1[:, t, :], scale=1.0, scalar=0.0,
                                           op0=ALU.mult, op1=ALU.add, accum_out=hdot[:, n % 2, k:k + 1]).then_inc(dots, 1)
                    if c:
                        if k == CHK * c:
                            gated(t, c - 1)
                        add_row(t, k - CHK)

            def do_last(t):
                gated(t, n_slots(t) // CHK - 1)
                for k in range(n_slots(t) - CHK, n_slots(t)):
                    add_row(t, k)

            def do_final(t):
                tn = TILES[t][1]
                dve.wait_ge(v_used, by_pe[slot_base[t] + n_slots(t) - 1] + (t < 2))
                dve.wait_ge(ln2_in, 16)
                for hf in range(2):
                    half = slice(512 * hf, 512 * hf + 512)
                    drain(("po", t, hf), V.scalar_tensor_tensor(out=x1[0:tn, t, half], in0=x1[0:tn, t, half], scalar=ALPHA,
                                                                in1=bank[6 + hf][0:tn, :], op0=ALU.mult, op1=ALU.add))
                layer_norm(x1[0:tn, t, :], x1[0:tn, t, :], tn, ln2).then_inc(y_s, 1)

            here = {"tables": do_tables, "wt": do_wt, "k": do_k, "ws": do_ws, "rec": do_rec, "qkv": do_qkv, "ss": do_ss, "pvs": do_pvs,
                    "s": do_s, "pv": do_pv, "merge": do_merge, "wo": do_wo, "wq": do_wq, "top": do_top, "choose": do_choose,
                    "peer": do_peer, "last": do_last, "final": do_final}
            for item in plan.items:
                if item[0] in here:
                    here[item[0]](*item[1:])

        @block.scalar
        def _(act):
            S = nc.scalar
            steps = [0]

            def step(ins):
                steps[0] += 1
                ins.then_inc(astep, 1)
                act.wait_ge(astep, steps[0])

            def drain(key, ins):
                who, n = plan.drained[key]
                ins.then_inc(drained["A"], 1)
                act.wait_ge(drained["A"], n)

            def full(key):
                act.wait_ge(filled, plan.filled[key])
                return bank[plan.bank[key]]

            def copy(out, in_):
                return S.activation(out, in_, ACT.Copy)

            def do_tables():
                act.dma_start(small[:, :], io["small"]).then_inc(small_in, 16)
                act.wait_ge(small_in, 16)
                step(S.activation(cx[:, 7, 0, :], s("ldt"), ACT.Exp))

            def do_u():
                for c, (c0, cn) in enumerate(GC0):
                    for m in range(4):
                        b = full(("u", c, m))
                        drain(("u", c, m), S.activation(uT[:, m, c0:c0 + cn], b[:, 0:cn], ACT.Identity, bias=s("bu")[:, m:m + 1]))

            def do_ut():
                for i in range(8):
                    b = full(("ut", i))
                    drain(("ut", i), copy(u_tok[0:CH, :, i, :], b[0:CH, :].rearrange("p (g c) -> p g c", c=GC)))

            def do_uc():
                for i in range(8):
                    b = full(("uc", i))
                    drain(("uc", i), copy(U[:, 4 * i:4 * i + 4, :].rearrange("p g n -> p (g n)"), b[:, 0:4 * CH]))

            def do_wt():
                for ri in range(2):
                    for i in (0, 2):
                        b = full(("wt", ri, i))
                        drain(("wt", ri, i), copy(Wm[:, ri, 4 * i:4 * i + 4, :].rearrange("p g n -> p (g n)"), b[:, :]))

            def do_k():
                for par in range(2):
                    for i in (0, 2):
                        b = full(("k", par, i))
                        drain(("k", par, i), copy(Kt[0:GC, 8 * i + par:8 * i + par + 7:2, :, :].rearrange("p g j c -> p g (j c)"),
                                                  b[0:GC, :].rearrange("p (g n) -> p g n", g=4)))

            def do_ws():
                for ri in range(2):
                    for i in (0, 2):
                        b = full(("ws", ri, i))
                        drain(("ws", ri, i), copy(Wst[:, ri, 4 * i:4 * i + 4, :].rearrange("p g n -> p (g n)"), b[:, 0:4 * CH]))

            def do_y(part):
                cn = CHUNKS[part][1]
                if part == 0:
                    act.wait_ge(toep_in, 16 * STEP)
                else:
                    act.wait_ge(filled, plan.filled[("ht", 0, 3, 1)])
                for par in range(2):
                    for i in range(4):
                        b = full(("y", part, par, i))
                        drain(("y", part, par, i), S.activation(y_tok[0:cn, :, 8 * i + par:8 * i + par + 7:2, :].rearrange("p j g c -> p g j c"),
                                                                b[0:cn, :].rearrange("p (g j c) -> p g j c", g=4, j=STEP), ACT.Gelu))

            def do_ht(part):
                c0, cn = CHUNKS[part]
                if part == 0:
                    wait_item(act, ("pv", 0, 1))
                    act.wait_ge(kv_out, 32)
                hg_view = hgT[:, :, :].rearrange("p m (n t) -> p m t n", t=STEP)
                for m in range(4):
                    for hf in range(2):
                        b = full(("ht", part, m, hf))
                        drain(("ht", part, m, hf), copy(hg_view[:, m, 4 * hf:4 * hf + 4, c0:c0 + cn],
                                                        b[:, 0:4 * cn].rearrange("p (t n) -> p t n", t=4)))

            def do_turn(t):
                t0, tn = TILES[t]
                b = full(("qt", t))
                if t == 0:
                    drain(("qt", t), copy(qs.rearrange("p b (h q) -> p h b q", h=HP),
                                          b[:, :].rearrange("p (h n) -> p h n", h=4)[:, :, 0:tn].rearrange("p h (b q) -> p h b q", q=STEP)))
                else:
                    c = 0 if t == 1 else rel(t)
                    drain(("qt", t), copy(qTg[group(t)][:, :, c:c + 128], b[:, :].rearrange("p (h n) -> p h n", h=4)))
                b = full(("kt", t))
                drain(("kt", t), copy(kT[:, t0:t0 + tn], b[:, 0:tn]))
                if t == 4:
                    act.wait_ge(roped, plan.index[("qkv", t)])
                    act.dma_start(io["kwp"], zt[4][:, 512:640]).then_inc(kv_out, 16)
                    act.dma_start(io["vwp"], zt[4][:, 640:768]).then_inc(kv_out, 16)
                if t == 0:
                    act.wait_ge(roped, plan.index[("qkv", t)])
                    for o, c in (("kws", 512), ("vws", 640)):
                        act.dma_start(io[o][:, WIN - STEP:WIN, :], zt[0][0:64, c:c + 128]).then_inc(kv_out, 16)

            def exponentials(n, scores, width):
                act.wait_ge(scored, n)
                step(S.activation(stat[:, 8:8 + width], stat[:, 8:8 + width], ACT.Exp))
                S.activation(scores, scores, ACT.Exp).then_inc(expd_s, 1)

            def do_ss():
                exponentials(1, Psm, 4)

            def do_pvs():
                PT = PTg[0]
                b = full(("spc",))
                drain(("spc",), copy(PT[:, 0].rearrange("p a b -> p (a b)"), b[:, :]))
                b = full(("spn",))
                drain(("spn",), copy(PT[0:64, 1].rearrange("p a b -> p (a b)"), b[0:64, :]))

            def do_s(j, kv):
                exponentials(1 + plan.index[("s", j, kv)], Pg[group(j + 1)], 4)

            def do_pv(j, kv):
                n, PT = plan.items.index(("pv", j, kv)), PTg[group(j + 1)]
                act.wait_ge(filled, max(plan.filled[k] for k in (("so",), *[("o", *i[1:]) for i in plan.items[:n] if i[0] == "pv"])))
                for i in range(2):
                    b = full(("pt", j, kv, i))
                    drain(("pt", j, kv, i), copy(PT[:, i].rearrange("p a b -> p (a b)"), b[:, :]))

            def do_gates(m):
                if m == 0:
                    wait_item(act, ("ws",))
                for i, what in enumerate(("gs", "ga")):
                    b = full((what, 0, m))
                    drain((what, 0, m), S.activation(sg[:, i, m], b[:, 0:192], ACT.Sigmoid, bias=s("b" + what)[:, m:m + 1]))

            def do_merge(g, m):
                n, cn = 8 * g + m, GC0[g][1]
                gt = gateg[g][:, n % 2, :, :]
                if m == 0:
                    wait_item(act, ("pv", 3 if g else 0, 1))
                if g and m == 0:
                    act.wait_ge(kv_out, 64)
                if m >= 2:
                    act.wait_ge(drained["D"], plan.drained[("up", g, m - 2)][1])
                for i, what in enumerate((("gs", "ga") if g else ()) + ("gb",)):
                    bias = s("bglu")[:, 8 + m:9 + m] if what == "gb" else s("b" + what)[:, m:m + 1]
                    b = full((what, g, m))
                    drain((what, g, m), S.activation(gt[:, i], b[:, 0:cn], ACT.Sigmoid, bias=bias))

            norms = [0]

            def deviation(tn):
                norms[0] += 1
                act.wait_ge(var_s, norms[0])
                S.activation(stat[0:tn, 79:80], stat[0:tn, 78:79], ACT.Sqrt).then_inc(std_s, 1)

            def do_wo(t):
                deviation(TILES[t][1])

            def do_xt(t):
                t0, tn = TILES[t]
                for hf in range(2):
                    b = full(("xt", t, hf))
                    drain(("xt", t, hf), copy(xT[:, 4 * hf:4 * hf + 4, t0:t0 + tn], b[:, :].rearrange("p (k n) -> p k n", k=4)[:, :, 0:tn]))

            def do_wq(g, h):
                if h % 2 == 0:
                    if h == 0:
                        wait_item(act, ("wo", GROUPS[g][-1]))
                    b = full(("wq", g, h))
                    drain(("wq", g, h), copy(q2Tg[g][:, h, :], b[:, 0:GC0[g][1]]))

            def do_choose(t, part):
                if part:
                    return
                n, tn = ORDER.index(t), TILES[t][1]
                act.wait_ge(sc_s, n + 1)
                S.activation(gts[0:tn, n % 2, :], gts[0:tn, n % 2, :], ACT.Exp).then_inc(sce_s, 1)

            def do_fold():
                n = ORDER.index(0)
                act.wait_ge(idx_s, n + 1)
                act.dma_start(idxf[0:64, :], idx[0:64, n % 2, 0:64]).then_inc(fold_in, 16)
                act.dma_start(idxf[64:128, :], idx[0:64, n % 2, 64:128]).then_inc(fold_in, 16)
                act.dma_start(gtf[0:64, :], gts[0:64, n % 2, 0:64]).then_inc(fold_in, 16)
                act.dma_start(gtf[64:128, :], gts[0:64, n % 2, 64:128]).then_inc(fold_in, 16)
                act.dma_start(x1[64:128, 0, :], x1[0:64, 0, :]).then_inc(fold_in, 16)

            done = [0]

            diag_slot = []

            def diagonals(t, c):
                n, tn, base = ORDER.index(t), TILES[t][1], slot_base[t]
                eye = s("fold") if t == 0 else ident
                done[0] += 1
                act.wait_ge(a_s, done[0])
                for k in range(CHK * c, CHK * c + CHK):
                    q = base + k
                    if on_dve[q]:
                        continue
                    d = q - by_dve[q]
                    if d >= DR:
                        act.wait_ge(v_used, by_pe[diag_slot[d - DR]])
                    diag_slot.append(q)
                    S.activation(diag[:, d % DR, 0:tn], eye, ACT.Copy, scale=aact[:, n % 2, k:k + 1]).then_inc(diag_s, 1)

            def do_peer(t, c):
                n, base = ORDER.index(t), slot_base[t]
                act.wait_ge(dots, base + CHK * c + CHK)
                k = slice(CHK * c, CHK * c + CHK)
                S.activation(hact[:, n % 2, k], hdot[:, n % 2, k], ACT.Gelu).then_inc(act_s, 1)

            def do_before(t, c):
                if c:
                    diagonals(t, c - 1)

            def do_last(t):
                diagonals(t, n_slots(t) // CHK - 1)

            def do_final(t):
                t0, tn = TILES[t]
                deviation(tn)
                act.wait_ge(y_s, ORDER.index(t) + 1)
                act.dma_start(io["y"][t0:t0 + tn, :], x1[0:tn, t, :]).then_inc(y_out, 16)

            here = {"tables": do_tables, "u": do_u, "ut": do_ut, "uc": do_uc, "wt": do_wt, "k": do_k, "ws": do_ws, "y": do_y, "ht": do_ht,
                    "turn": do_turn, "ss": do_ss, "pvs": do_pvs, "s": do_s, "pv": do_pv, "gates": do_gates, "merge": do_merge,
                    "wo": do_wo, "xt": do_xt, "wq": do_wq, "choose": do_choose, "fold": do_fold, "before": do_before, "peer": do_peer, "last": do_last,
                    "final": do_final}
            for item in mixer_first(plan.items):
                if item[0] in here:
                    here[item[0]](*item[1:])
            act.wait_ge(y_out, 16 * 5)
            act.wait_ge(kv_out, 16 * 4)
            act.wait_ge(ssm_out, 16)
            act.wait_ge(win_out, 16 * 2)


def packed_inputs(I):
    f = lambda n: np.asarray(I[n])[0]
    x = np.concatenate([np.asarray(I["x_sample"]).reshape(64, DM), np.asarray(I["x_prompt"]).reshape(SEQ, DM)])
    order = [kv * HP + hp for hp in range(HP) for kv in range(NKV)]
    w_in, b_in = f("w_in"), f("b_in")
    wu, wq, wkv, wgs, wga = np.split(w_in, [512, 1024, 1280, 2304], axis=1)
    bu, bq, bkv, bgs, bga = np.split(b_in, [512, 1024, 1280, 2304])
    wq = wq.reshape(DM, NH, HD)[:, order].reshape(DM, 512)
    bq = bq.reshape(NH, HD)[order].reshape(512)
    kmaj = lambda w: w.reshape(-1, 128, w.shape[1]).transpose(1, 0, 2)
    wu, wq, wkv, wgs, wga = (kmaj(w) for w in (wu, wq, wkv, wgs, wga))
    glu, up = kmaj(f("w_glu")), kmaj(f("w_attn_up").reshape(NH, HD, DM)[order].reshape(512, DM))
    wo, wpq = kmaj(f("w_out")), kmaj(f("peer_wq"))
    cols = lambda w, m: w[:, :, 128 * m:128 * m + 128]
    cut = {"u": lambda i: cols(wu, i), "q": lambda i: wq[:, 2 * i:2 * i + 2], "kv": lambda i: wkv[:, 4 * i:4 * i + 4],
           "gs": lambda i: cols(wgs, i), "ga": lambda i: cols(wga, i),
           "glu": lambda i: np.concatenate([cols(glu, i), cols(glu, 8 + i)], 1),
           "up": lambda i: np.concatenate([cols(up, 2 * i), cols(up, 2 * i + 1)], 1),
           "wo": lambda i: wo[:, i], "wq": lambda i: cols(wpq, i)}
    w = np.stack([cut[k](i).reshape(128, 1024) for _, k, i in Plan().pieces])

    def pairs(a):
        a = a.reshape(GP, 2, NS, *a.shape[2:])
        return np.moveaxis(a, 0, 2).reshape(128, GP, *a.shape[3:])

    freqs = np.float32(500000.0) ** (-np.arange(0, ROPE, 2, dtype=np.float32) / np.float32(ROPE))
    pos = np.concatenate([np.tile(PAST + np.arange(STEP), NSEQ), np.arange(SEQ)]).astype(np.float32)
    ang = (pos[:, None] * freqs[None, :]).astype(np.float32)
    tab = np.stack([np.cos(ang.astype(np.float64)), np.sin(ang.astype(np.float64))], 1).astype(np.float32)
    rope = np.zeros((128, 5, 2, 8), np.float32)
    for t, (t0, tn) in enumerate(TILES):
        rope[:tn, t] = tab[t0:t0 + tn]
    q, k = np.arange(128)[:, None], np.arange(256)[None, :]
    maskp = np.where((128 + q - k >= 0) & (128 + q - k < WIN), 0.0, NEG).astype(np.float32)
    masks = np.full((128, 2, WIN + 64), NEG, np.float32)
    row = np.arange(128)
    for hf in range(2):
        b, st = 4 * hf + row // 32, row % 8
        masks[:, hf, :WIN][st[:, None] < np.arange(WIN)[None, :]] = 0.0
        new = np.arange(64)[None, :]
        masks[:, hf, WIN:][(new // 8 == b[:, None]) & (new % 8 <= st[:, None])] = 0.0
    rep = lambda v: np.broadcast_to(v, (128, v.size))
    per = lambda v: v.reshape(-1, 128).T
    sinks = f("attn_sinks")
    sink_rows = np.stack([sinks[4 * kv + (row // 8) % 4] for kv in range(2)], 1)
    re, im = (np.asarray(I[n])[0].transpose(1, 2, 0) for n in ("state_ssm_re", "state_ssm_im"))
    dsk = np.zeros((128, G * GC), np.float32)
    parts = {
        "ident": np.eye(128, dtype=np.float32), "fold": np.tile(np.eye(64, dtype=np.float32), (2, 1)),
        "are": pairs(f("ssm_a_re")), "aim": pairs(f("ssm_a_im")),
        "ldt": pairs(np.broadcast_to(f("ssm_log_dt")[:, None], (G, NS))),
        "bb": np.stack([pairs(f("ssm_b_re")), pairs(f("ssm_b_im"))], 1),
        "cc": np.stack([pairs(f("ssm_c_re").transpose(0, 2, 1)), pairs(f("ssm_c_im").transpose(0, 2, 1))], 1),
        "k12": np.concatenate([f("peer_k1").transpose(2, 0, 1), f("peer_k2").transpose(2, 0, 1)]),
        "maskp": maskp, "masks": masks, "rope": rope, "h0": np.stack([pairs(re), pairs(im)], 1),
        "bu": per(bu), "bgs": per(bgs), "bga": per(bga), "bglu": per(f("b_glu")),
        "sinkp": rep(sinks), "sinks": sink_rows, "dskip": rep(f("ssm_d")), "iota": rep(np.arange(TOPK, dtype=np.float32)),
        "bqkv": rep(np.concatenate([bq, bkv])),
    }
    small = np.concatenate([np.ascontiguousarray(parts[n]).reshape(128, wd) for n, wd in _SMALL], 1)
    ck, cv = np.asarray(I["cache_k_win"])[0], np.asarray(I["cache_v_win"])[0]
    lnp = np.concatenate([rep(f(n)) for n in ("ln1_g", "ln1_b", "ln2_g", "ln2_b")], 1)
    out = {"small": small, "xT": x.T, "x": x, "w": w, "lnp": lnp,
           "kcT": ck.transpose(2, 3, 0, 1).reshape(128, NSEQ, WIN), "vc": cv.transpose(1, 0, 2, 3).reshape(WIN, NSEQ, 128),
           "ckn": ck.reshape(NSEQ, WIN, 128), "cvn": cv.reshape(NSEQ, WIN, 128), "pu": f("peer_u"), "pv": f("peer_v")}
    return {k: np.ascontiguousarray(v) for k, v in out.items()}


OUTS = {"y": (TOK, DM), "kwp": (WIN, 128), "vwp": (WIN, 128), "kws": (NSEQ, WIN, 128), "vws": (NSEQ, WIN, 128),
        "ssm": (128, 2 * GP * (1 + NSEQ))}


def kernel(**inputs):
    import concourse.bacc as bacc
    from concourse.bass_utils import run_bass_kernel_spmd

    nc = bacc.Bacc("TRN2", target_bir_lowering=False, num_devices=1)
    arrays, io = {}, {}
    for name, a in packed_inputs(inputs).items():
        arrays["in_" + name] = a
        io[name] = nc.dram_tensor("in_" + name, a.shape, mybir.dt.from_np(a.dtype), kind="ExternalInput").ap()
    for name, shape in OUTS.items():
        io[name] = nc.dram_tensor("out_" + name, shape, F32, kind="ExternalOutput").ap()
    hybrid_step(nc, io)
    r = run_bass_kernel_spmd(nc, [arrays], core_ids=[0]).results[0]
    y = r["out_y"]
    ssm = r["out_ssm"].reshape(2, NS, 2, GP, 1 + NSEQ).transpose(2, 4, 3, 0, 1).reshape(2, 1 + NSEQ, G, NS)
    win = lambda n, b: r["out_" + n].reshape(1, b, WIN, NKV, HD)
    return (y[64:].reshape(1, SEQ, DM), y[:64].reshape(NSEQ, STEP, DM), win("kwp", 1), win("vwp", 1),
            ssm[0:1, 0:1], ssm[1:2, 0:1], win("kws", NSEQ), win("vws", NSEQ), ssm[0:1, 1:], ssm[1:2, 1:])
```

```python
import math
from contextlib import ExitStack

import numpy as np

import concourse.bass as bass
from concourse import mybir

F32, U32 = mybir.dt.float32, mybir.dt.uint32
ALU, ACT = mybir.AluOpType, mybir.ActivationFunctionType
AX = mybir.AxisListType.X

DM, SEQ, NSEQ, STEP, PAST = 1024, 512, 8, 8, 1024
SSM, G, GC, NS = 512, 32, 16, 64
NH, NKV, HD, WIN, ROPE = 8, 2, 64, 128, 16
HP = NH // NKV
NE, KEYS, TOPK, HALF = 16384, 128, 16, 64
TOK = NSEQ * STEP + SEQ
CH = TOK // STEP
GP = G // 2
KT = DM // 128
ALPHA, EPS, NEG = 2.0 ** 0.25, 1e-5, -1e30
TILES = [(0, 64)] + [(64 + 128 * j, 128) for j in range(4)]
GROUPS = [[1, 0], [2, 3, 4]]
COLS = [(0, 192), (192, 384)]
FIRST = 24
ORDER = [1, 0, 2, 3, 4]
PIECES = 8
EARLY = 72
U_PLACES = ([0, 1, 2, 3, 4, 5], [0, 1, 2, 3], [0, 1, 2, 3] + list(range(6, 12)))
V_PLACES = ([0, 1, 2, 3, 4, 5, 6, 7, 8], [0, 1, 2, 3, 4, 5], [0, 1, 2, 3, 4, 5] + list(range(9, 15)))
V_LAG = 4
V_SHARE = {1: [1] * 3 + [3] * 3 + [6] * 10, 0: [6] * 3 + [3] * 2 + [0] * 3}
TOPS_AT = (9, 10, 12, 14, 16, 18, 20, 22, 24, 25)
LATE_AT = 1
DIAGS = 8
STEP_SLOTS = 4

_SMALL = [("bu", 4), ("ident", 128), ("fold", 64), ("are", GP), ("aim", GP), ("ldt", GP), ("bb", 2 * GP * GC),
          ("cc", 2 * GP * GC), ("k12", NH * KEYS), ("maskp", 2 * WIN),
          ("h0", 2 * GP * NSEQ), ("dskip", G * GC), ("masks", 2 * (WIN + 64)), ("rope", 5 * ROPE), ("bgs", 8), ("bga", 8), ("bglu", 16),
          ("sinkp", NH), ("sinks", NKV), ("iota", TOPK), ("bqkv", 768)]
SM, _c = {}, 0
for _n, _w in _SMALL:
    SM[_n] = (_c, _c + _w)
    _c += _w
SMC = _c


def n_slots(t):
    return 64 if t == 0 else 128


def schedule():
    s = [("tables",), ("u",), ("ut",), ("uc",), ("qkv", 0), ("qkv", 1), ("turn", 0), ("turn", 1), ("wt",), ("k",), ("ws",),
         ("rec",), ("ss",), ("gates", 0, 0), ("gates", 0, 1), ("pvs",), ("s", 0, 0), ("gates", 0, 2), ("gates", 0, 3), ("pv", 0, 0),
         ("s", 0, 1), ("gates", 0, 4), ("gates", 0, 5), ("pv", 0, 1), ("gates", 0, 6), ("gates", 0, 7), ("y", 0), ("y", 1), ("ht",)]
    s += [("merge", 0, m) for m in range(8)]
    s += [("wo", 1), ("wo", 0), ("xt", 1), ("xt", 0)] + [("wq", 0, h) for h in range(4)] + [("sc", 1, 0)]
    s += [("wq", 0, h) for h in range(4, 8)]
    s += [("top", 1, h) for h in range(4)] + [("sc", 1, 1), ("choose", 1, 0)]
    first = [[("top", 1, h)] for h in range(4, 8)] + [[("choose", 1, 1)]]
    tops = [[("sc", 0, 0), ("top", 0, 0)]] + [[("top", 0, h)] for h in (1, 2, 3)] + [[("choose", 0, 0)], [("sc", 0, 1), ("top", 0, 4)]]
    tops += [[("top", 0, h)] for h in (5, 6, 7)] + [[("choose", 0, 1), ("fold",)]]
    mix = [[("qkv", 2)], [("qkv", 3)], [("qkv", 4)], [("turn", 2), ("turn", 3), ("turn", 4), ("s", 1, 0)]]
    parts = [(j, kv) for j in range(1, 4) for kv in range(2)]
    for n, (j, kv) in enumerate(parts):
        mix.append([("pv", j, kv)] + ([("s", *parts[n + 1])] if n + 1 < len(parts) else []))
    for m in range(8):
        mix += [[("gates", 1, m)], [("merge", 1, m)]]
    mix += [[("wo", 2)], [("wo", 3), ("xt", 2)], [("wo", 4), ("xt", 3)], [("xt", 4), ("wq", 1, 0)]]
    mix += [[("wq", 1, h)] for h in range(1, 8)]
    mix += [[("sc", 2, 0), ("sc", 2, 1), ("top", 2, 0)]] + [[("top", 2, h)] for h in (1, 2, 3)]
    mix += [[("choose", 2, 0)]]
    late = [("top", 2, h) for h in range(4, 8)] + [("choose", 2, 1)]
    b = []
    for n, entry in enumerate(mix):
        b.append((first.pop(0) if first else []) + entry + (tops.pop(0) if n in TOPS_AT else []))
    assert not tops
    steps = [("peer", t, c) for t in ORDER[:2] for c in range(n_slots(t) // STEP_SLOTS)]
    per, at = len(b) / len(steps), 0.0
    for t in ORDER:
        n = n_slots(t) // STEP_SLOTS
        nxt = [("sc", t + 1, 0), ("sc", t + 1, 1)] + [("top", t + 1, h) for h in range(4)] + [("choose", t + 1, 0)]
        nxt += [("top", t + 1, h) for h in range(4, 8)] + [("choose", t + 1, 1)]
        for c in range(n):
            s.append(("peer", t, c))
            if c == 0 and t != ORDER[0]:
                s.append(("final", ORDER[ORDER.index(t) - 1]))
            if t in ORDER[:2]:
                at += per
                while b and at >= 1 - 1e-9:
                    s += b.pop(0)
                    at -= 1
            elif late and c >= LATE_AT:
                s.append(late.pop(0))
            elif t < 4 and c >= 6 and c % 2 == 0 and nxt:
                s.append(nxt.pop(0))
        s.append(("last", t))
        if t == ORDER[1]:
            for x in b:
                s += x
    s.append(("final", ORDER[-1]))
    return s


def mixer_first(items):
    out, held = [], None
    for item in items:
        if item[0] in ("peer", "last") and held:
            out.append(held)
            held = None
        if item[0] == "peer":
            held = item
            out.append(("before", *item[1:]))
        else:
            out.append(item)
    return out + ([held] if held else [])


def item_jobs(item):
    k, a, ad = item[0], item[1:], "AD"
    if k == "u":
        return [(("u", c, m), "A", [("u", m)]) for c in range(2) for m in range(4)]
    if k in ("ut", "uc"):
        return [((k, i), "A", []) for i in range(8)]
    if k in ("wt", "k", "ws"):
        return [((k, i // 4, i % 4), ad[i % 2], []) for i in range(8)]
    if k == "y":
        return [(("y", *a, i), "A", []) for i in range(4)]
    if k == "ht":
        return [(("ht", i // 2, i % 2), "A", []) for i in range(8)]
    if k == "qkv":
        g = a[0] > 1
        return [(("q", a[0]), "D", [(g, "q", i) for i in range(4)]), (("kv", a[0]), "D", [(g, "kv", i) for i in range(2)])]
    if k == "turn":
        return [(("qt", a[0]), "A", []), (("kt", a[0]), "A", [])]
    if k == "ss":
        return [(("ss", i // 2, i % 2), "D", []) for i in range(4)]
    if k == "pvs":
        return [(("spc",), "A", []), (("spn",), "A", []), (("so",), "D", [])]
    if k == "s":
        return [(("s", *a, hf), "D", []) for hf in range(2)]
    if k == "pv":
        return [(("pt", *a, i), "A", []) for i in range(2)] + [(("o", *a), "D", [])]
    if k == "gates":
        return [((w, *a), "A", [(a[0], w, a[1])]) for w in ("gs", "ga")]
    if k == "merge":
        g, m = a
        return [(("gb", g, m), "A", [(g, "glu", m)]), (("gl", g, m), "D", [(g, "glu", m)]), (("up", g, m), "D", [(g, "up", m // 2)])]
    if k == "wo":
        return [(("wo", a[0], hf), "D", [(a[0] > 1, "wo", i) for i in range(8)]) for hf in range(2)]
    if k == "xt":
        return [(("xt", a[0], hf), "A", []) for hf in range(2)]
    if k == "wq":
        return [(("wq", *a), ad[a[1] % 2] if a[0] else "A", [(a[0], "wq", a[1])])]
    if k == "sc":
        return [(("sc", a[0], side, a[1]), "S", []) for side in range(2)]
    if k == "last":
        return [(("po", a[0], hf), "D", []) for hf in range(2)]
    return []


class Plan:

    def __init__(self):
        self.items = schedule()
        self.filled, self.drained, self.before, self.bank = {}, {}, {}, {}
        self.passed, self.index, self.pieces, self.last_use = {}, {}, [], {}
        scores = self.items.index(("sc", ORDER[0], 0))
        scores_read = 0
        last, n, counts, turn, kinds = {}, 0, {"D": 0, "A": 0, "S": 0}, 0, {}
        for at, item in enumerate(self.items):
            kinds[item[0]] = kinds.get(item[0], 0) + 1
            self.index[item] = kinds[item[0]]
            for key, who, pieces in item_jobs(item):
                if key[0] == "po":
                    bank = 6 + key[2]
                elif key[0] == "sc":
                    bank = key[2] + (4 if key[3] == 0 or key[1] < 2 else 2)
                elif at < scores:
                    bank, turn = turn % 8, turn + 1
                else:
                    bank, turn = turn % 4, turn + 1
                n += key[0] != "po"
                counts[who] += 1
                self.filled[key], self.drained[key], self.bank[key] = n, (who, counts[who]), bank
                self.before[key] = last.get(bank)
                last[bank] = (who, counts[who])
                for p in pieces:
                    p = (int(p[0]), *p[1:]) if len(p) == 3 else (0, *p)
                    if p not in self.last_use:
                        self.pieces.append(p)
                    self.last_use[p] = key
            if item[0] == "top" and item[2] % 4 == 3:
                scores_read += 2
            self.passed[item] = (n, counts["D"], counts["A"], scores_read)


def hybrid_step(nc, io):
    plan = Plan()
    pieces = plan.pieces
    piece_no = {p: i for i, p in enumerate(pieces)}

    ctx = ExitStack()
    with ctx:
        def sb(name, shape, dt=F32):
            return ctx.enter_context(nc.sbuf_tensor(name, shape, dt))

        def sem(name):
            return ctx.enter_context(nc.semaphore(name))

        wring = sb("wring", [128, PIECES, 1024])
        small = sb("small", [128, SMC])
        xT = sb("xT", [128, KT, TOK])
        hgT = sb("hgT", [128, 4, TOK])
        R = sb("region", [128, 31944])
        fin = sb("fin", [128, 2, GP, 1 + NSEQ])
        disc = sb("discretisation", [128, 1120])
        cx = disc[:, 0:320].rearrange("p (a b c) -> p a b c", a=10, b=2)
        stat = sb("stat", [128, 80])
        Bb = disc[:, 320:832].rearrange("p (a b c) -> p a b c", a=2, b=GP)
        pw = disc[:, 832:1120].rearrange("p (a b c) -> p a b c", a=2, b=GP)
        a8 = sb("a8", [128, 2, 2, GP])

        def s(name, *dims):
            a, b = SM[name]
            v = small[:, a:b]
            if len(dims) == 2:
                v = v.rearrange("p (a b) -> p a b", a=dims[0])
            if len(dims) == 3:
                v = v.rearrange("p (a b c) -> p a b c", a=dims[0], b=dims[1])
            return v

        def view(at, *dims):
            v = R[:, at:at + math.prod(dims)]
            if len(dims) == 2:
                v = v.rearrange("p (a b) -> p a b", a=dims[0])
            if len(dims) == 3:
                v = v.rearrange("p (a b c) -> p a b c", a=dims[0], b=dims[1])
            if len(dims) == 4:
                v = v.rearrange("p (a b c d) -> p a b c d", a=dims[0], b=dims[1], c=dims[2])
            return v

        ident = s("ident")
        AB = view(0, 2, GP, STEP, GC)
        T1, T2 = view(4096, 8, 9, GC), view(4096 + 1152, 8, 9, GC)
        CA = view(6400, 2, GP, 9, GC)
        Wm = view(11008, 2, GP, 128)
        Tm = view(15104, G, 128)
        u_tok = view(19200, G, STEP, GC)
        y_tok = view(19200, STEP, G, GC)
        Kt = view(19200, G, STEP, GC)
        uT = view(23296, 4, TOK)
        U = view(25600, G, CH)
        H = view(27904, 2, GP, CH + 1)
        Wst = view(0, 2, GP, CH)
        eye_d, st1, st2 = view(5376, G, GC), view(5888, 2, GP, NSEQ), view(6144, 2, GP, NSEQ)
        early = hgT[:, :, :].rearrange("p a b -> p (a b)")
        zt = [early[:, 0:768]] + [view(a, 768) for a in (30240, 23936, 24704, 25472)]
        qs = early[:, 768:1024].rearrange("p (b n) -> p b n", b=NSEQ)
        qTg = [early[:, 1024:1536].rearrange("p (h n) -> p h n", h=4), view(26240, 4, 384)]
        oTg = [view(4352, 4, 192), view(26240, 4, 384)]
        kT, rt = view(31008, TOK), view(31584, 4, 10, 8)
        Pg, Psm = [view(2304, 4, 2 * WIN), view(27776, 4, 2 * WIN)], view(2304, 4, WIN + 64)
        PTg = [view(3328, 2, 4, 128), view(28800, 2, 4, 128)]
        kc, vc = view(23296, NSEQ, WIN), view(23296 + 1024, NSEQ, WIN)
        sg = view(11008, 2, 8, 192)
        gateg = [view(2304, 2, 1, 192), view(23936, 2, 3, 384)]
        partg = [view(2688, 2, 192), view(30848, 2, 384)]
        mTg = [view(23296, KT, 192), view(27776, KT, 384)]
        q2P0, q2B = view(23296, NH, WIN), view(23936, NH, 384)

        def q2T(t, h):
            if t > 1:
                return q2B[:, h, rel(t):rel(t) + TILES[t][1]]
            return q2P0[:, h, :] if t else hgT[:, h // 2, 64 * (h % 2):64 * (h % 2) + 64]

        ln1, ln2 = view(11008, 2, DM), view(18176, 2, DM)
        x1 = [view(a, DM) for a in (0, 1024, 15104, 16128, 17152)]
        early_rows = [view(15104 + 1024 * i, DM) for i in range(5)]
        ring_u = [view(5888 + 1024 * i, DM) for i in range(4)] + early_rows[0:2] + [wring[:, i, :] for i in range(6)]
        ring_v = [view(a, DM) for a in (9984, 20224, 21248, 22272)] + [disc[:, 0:DM], small[:, SM["h0"][0]:SM["h0"][0] + DM]] + \
                 early_rows[2:5] + [wring[:, 6 + i, :] for i in range(2)] + [view(27008 + 1024 * i, DM) for i in range(4)]
        diag = small[:, SM["bb"][0]:SM["cc"][1]].rearrange("p (a b) -> p a b", a=DIAGS)
        cand = view(13056, TOPK, TOPK)
        eq = view(13056, NH * TOPK // 2, TOPK)
        acc = view(14080, DM)
        scr = view(2048, 256)
        v16, i16f = view(2304, 2, NH, TOPK), view(2560, 2, NH, TOPK)
        top = view(2816, NH, TOPK)
        posf, ef = view(2944, 2, NH * TOPK), view(3200, 2, NH * TOPK)
        gts, gtf = view(3456, 2, 128), view(3712, 64)
        hdot, hact, aact = view(3776, 2, 128), view(4032, 2, 128), view(4288, 2, 128)
        i16 = view(4544, 2, NH, TOPK).bitcast(U32)
        pos = view(4800, NH, TOPK).bitcast(U32)
        pos2 = view(4928, 2, NH * TOPK).bitcast(U32)
        idx, idxf = view(5184, 2, 128).bitcast(U32), view(5440, 64).bitcast(U32)

        bank = [ctx.enter_context(nc.psum_tensor(f"bank{i}", [128, 512], F32)) for i in range(8)]

        filled = sem("bank_filled")
        drained = {"D": sem("bank_drained_by_vector"), "A": sem("bank_drained_by_scalar"), "S": sem("scores_read_by_vector")}
        w_here = [sem(f"weights_in_slot{i}") for i in range(PIECES)]
        small_in, xT_in, caches_in, x_in, ln_in = (sem(n) for n in ("small_in", "xT_in", "caches_in", "x_in", "ln_in"))
        tables_in = sem("ssm_parameters_in")
        xT2_in, x2_in, ln2_in = sem("xT2_in"), sem("x2_in"), sem("ln2_in")
        vstep, astep, pstep = sem("vector_step"), sem("scalar_step"), sem("gpsimd_step")
        tables_ready = sem("ssm_tables_ready")
        toep_zero = sem("toeplitz_zeroed")
        kernel_ready = sem("impulse_response_ready")
        toep_in = sem("toeplitz_placed")
        states_ready, later_states = sem("chunk_states_ready"), sem("later_chunk_states_ready")
        roped = sem("rotary_done")
        scored = sem("scores_masked")
        expd_s = sem("exponentials_ready")
        probs = sem("probabilities_ready")
        sig = sem("gates_ready")
        merged = sem("merged_part_ready")
        var_s, std_s = sem("variance_ready"), sem("deviation_ready")
        x1_s = sem("x1_tile_ready")
        sc_s, sce_s = sem("top_scores_ready"), sem("top_exponentials_ready")
        idx_s = sem("expert_indices_ready")
        fold_in = sem("folded_sample_in")
        g_u = [sem(f"u_rows_in{i}") for i in range(len(ring_u))]
        g_v = [sem(f"v_rows_in{i}") for i in range(len(ring_v))]
        dots, v_used, v_used_d = sem("u_dot_done"), sem("v_rows_used"), sem("v_rows_used_by_vector")
        act_s, a_s, diag_s = sem("gelu_ready"), sem("activation_ready"), sem("diagonal_ready")
        y_s, y_out = sem("y_tile_ready"), sem("y_stored")
        kv_out, ssm_out, win_out = sem("kv_stored"), sem("ssm_stored"), sem("cached_window_stored")

        block = ctx.enter_context(nc.Block())

        def wait_item(eng, item):
            f, d, a, sc = plan.passed[item]
            eng.wait_ge(filled, f)
            eng.wait_ge(drained["D"], d)
            eng.wait_ge(drained["A"], a)
            if sc:
                eng.wait_ge(drained["S"], sc)

        def group(t):
            return int(t > 1)

        def rel(t):
            return TILES[t][0] - COLS[group(t)][0]

        slot_base, by_pe, by_dve, on_dve = {}, [], [], []
        for t in ORDER:
            slot_base[t] = len(on_dve)
            share = V_SHARE.get(t, [0] * (n_slots(t) // 8))
            for k in range(n_slots(t)):
                on_dve.append((k % 8 + 1) * share[k // 8] // 8 > k % 8 * share[k // 8] // 8)
                by_dve.append(sum(on_dve))
                by_pe.append(len(on_dve) - by_dve[-1] + min(len(slot_base) - 1, 2))

        class Ring:
            def __init__(self, places):
                self.place, self.nth, self.before, holds = [], [], [], {}
                for q in range(len(on_dve)):
                    part, first = (0, 0) if q < EARLY else (1, EARLY) if q < slot_base[2] else (2, slot_base[2])
                    p = places[part][(q - first) % len(places[part])]
                    self.before.append(holds.get(p))
                    self.nth.append(self.nth[holds[p]] + 1 if p in holds else 1)
                    self.place.append(p)
                    holds[p] = q

        u_at, v_at = Ring(U_PLACES), Ring(V_PLACES)

        def wait_v_used(eng, q):
            eng.wait_ge(v_used_d if on_dve[q] else v_used, by_dve[q] if on_dve[q] else by_pe[q])

        @block.sync
        def _(sp):
            xv = io["xT"].rearrange("(k p) n -> p k n", p=128)
            sp.dma_start(xT[:, :, 0:192], xv[:, :, 0:192]).then_inc(xT_in, 16)
            for i, p in enumerate(pieces):
                if i == 1:
                    sp.dma_start(xT[:, :, 192:TOK], xv[:, :, 192:TOK]).then_inc(xT2_in, 16)
                if i >= PIECES:
                    sp.wait_ge(filled, plan.filled[plan.last_use[pieces[i - PIECES]]])
                if p == (1, "wo", 0):
                    wait_item(sp, ("sc", 0, 1))
                    sp.wait_ge(dots, EARLY)
                    sp.wait_ge(v_used, by_pe[EARLY - 1])
                    sp.wait_ge(v_used_d, by_dve[EARLY - 1])
                    sp.dma_start(ln2, io["lnp"].rearrange("p (a b) -> p a b", a=4)[:, 2:4, :]).then_inc(ln2_in, 16)
                    for t in GROUPS[1]:
                        t0, tn = TILES[t]
                        sp.dma_start(x1[t][0:tn, :], io["x"][t0:t0 + tn, :]).then_inc(x2_in, 16)
                sp.dma_start(wring[:, i % PIECES, :], io["w"][i]).then_inc(w_here[i % PIECES], 16)

        @block.gpsimd
        def _(pool):
            nc.gpsimd.memset(Tm[:, :, :], 0.0).then_inc(toep_zero, 1)
            for c, o in (("ckn", "kws"), ("cvn", "vws")):
                pool.dma_start(io[o][:, 0:WIN - STEP, :], io[c][:, STEP:WIN, :]).then_inc(win_out, 16)
            wait_item(pool, ("ut",))
            pool.dma_start(kc, io["kcT"]).then_inc(caches_in, 16)
            pool.dma_start(vc, io["vc"]).then_inc(caches_in, 16)
            pool.wait_ge(toep_zero, 1)
            pool.wait_ge(kernel_ready, 1)
            for i in range(STEP):
                pool.dma_start(Tm[16 * i:16 * i + 16, :, GC * i:128],
                               Kt.rearrange("p g j c -> p g (j c)")[0:16, :, 0:128 - GC * i]).then_inc(toep_in, 16)
            p1, p2 = cx[:, 2, :, :], cx[:, 3, :, :]
            wait_item(pool, ("ws",))
            pool.wait_ge(states_ready, 1)
            steps = 0
            for c in range(FIRST, CH):
                nc.gpsimd.tensor_tensor(p1, H[:, :, :, c], a8[:, 0], ALU.mult).then_inc(pstep, 1)
                nc.gpsimd.tensor_tensor(p2, H[:, 1::-1, :, c], a8[:, 1], ALU.mult).then_inc(pstep, 1)
                pool.wait_ge(pstep, steps + 1)
                nc.gpsimd.tensor_tensor(p1, p1, Wst[:, :, :, c], ALU.add).then_inc(pstep, 1)
                pool.wait_ge(pstep, steps + 3)
                last = nc.gpsimd.tensor_tensor(H[:, :, :, c + 1], p1, p2, ALU.add)
                if c < CH - 1:
                    last.then_inc(pstep, 1)
                    steps += 4
                    pool.wait_ge(pstep, steps)
            last.then_inc(later_states, 1)
            pool.wait_ge(later_states, 1)
            steps += 3
            nc.gpsimd.tensor_copy(fin[:, :, :, 0], H[:, :, :, CH]).then_inc(pstep, 1)
            nc.gpsimd.tensor_tensor(st1, H[:, :, :, 0:NSEQ], a8[:, 0].unsqueeze(3).broadcast_to([128, 2, GP, NSEQ]), ALU.mult).then_inc(pstep, 1)
            nc.gpsimd.tensor_tensor(st2, H[:, 1::-1, :, 0:NSEQ], a8[:, 1].unsqueeze(3).broadcast_to([128, 2, GP, NSEQ]),
                                    ALU.mult).then_inc(pstep, 1)
            pool.wait_ge(pstep, steps + 3)
            nc.gpsimd.tensor_tensor(st1, st1, st2, ALU.add).then_inc(pstep, 1)
            pool.wait_ge(pstep, steps + 4)
            nc.gpsimd.tensor_tensor(fin[:, :, :, 1:1 + NSEQ], st1, Wst[:, :, :, 0:NSEQ], ALU.add).then_inc(later_states, 1)
            pool.wait_ge(later_states, 2)
            pool.dma_start(io["ssm"], fin[:, :, :, :].rearrange("p a b c -> p (a b c)")).then_inc(ssm_out, 16)
            for t in GROUPS[0]:
                t0, tn = TILES[t]
                pool.dma_start(x1[t][0:tn, :], io["x"][t0:t0 + tn, :]).then_inc(x_in, 16)
            wait_item(pool, ("merge", 0, 7))
            pool.dma_start(ln1, io["lnp"].rearrange("p (a b) -> p a b", a=4)[:, 0:2, :]).then_inc(ln_in, 16)
            wait_item(pool, ("ht",))
            for n, t in enumerate(ORDER):
                ns, base = n_slots(t), slot_base[t]
                if t == 0:
                    pool.wait_ge(fold_in, 16 * 5)
                if t == 2:
                    wait_item(pool, ("wq", 1, 7))
                ind = idxf if t == 0 else idx[:, n % 2, :]

                def u_row(k):
                    q = base + k
                    if k == 0:
                        pool.wait_ge(idx_s, 2 * n + (2 if t == 0 else 1))
                    if k == 64:
                        pool.wait_ge(idx_s, 2 * n + 2)
                    if u_at.before[q] is not None:
                        pool.wait_ge(dots, u_at.before[q] + 1)
                    pool.indirect_dma_start(ring_u[u_at.place[q]], None, io["pu"],
                                            bass.IndirectOffsetOnAxis(ind[:, k:k + 1], 0)).then_inc(g_u[u_at.place[q]], 16)

                def v_row(k):
                    q = base + k
                    if v_at.before[q] is not None:
                        wait_v_used(pool, v_at.before[q])
                    pool.indirect_dma_start(ring_v[v_at.place[q]], None, io["pv"],
                                            bass.IndirectOffsetOnAxis(ind[:, k:k + 1], 0)).then_inc(g_v[v_at.place[q]], 16)

                for k in range(ns):
                    u_row(k)
                    if k >= V_LAG:
                        v_row(k - V_LAG)
                for k in range(ns - V_LAG, ns):
                    v_row(k)

        @block.tensor
        def _(pe):
            def enter(key):
                if plan.before[key]:
                    who, n = plan.before[key]
                    pe.wait_ge(drained[who], n)
                return bank[plan.bank[key]]

            def after(key):
                who, n = plan.drained[key]
                pe.wait_ge(drained[who], n)

            def arrived(*p):
                i = piece_no[p]
                pe.wait_ge(w_here[i % PIECES], 16 * (i // PIECES + 1))
                return wring[:, i % PIECES, :]

            mm, tr = nc.tensor.matmul, nc.tensor.transpose

            def do_u():
                for c, (c0, cn) in enumerate(COLS):
                    pe.wait_ge(xT2_in if c else xT_in, 16)
                    for m in range(4):
                        b = enter(("u", c, m))
                        w = arrived(0, "u", m).rearrange("p (k n) -> p k n", k=KT)
                        for k in range(KT):
                            last = mm(b[:, 0:cn], w[:, k, :], xT[:, k, c0:c0 + cn], start=k == 0, stop=k == KT - 1)
                        last.then_inc(filled, 1)

            def do_ut():
                pe.wait_ge(small_in, 16)
                after(("u", 1, 3))
                for i in range(STEP):
                    b = enter(("ut", i))
                    for m in range(4):
                        last = tr(b[0:CH, 128 * m:128 * m + 128], uT[:, m, i::STEP], ident)
                    last.then_inc(filled, 1)

            def do_uc():
                after(("ut", 7))
                for i in range(8):
                    b = enter(("uc", i))
                    for g in range(4):
                        last = tr(b[:, CH * g:CH * g + CH], u_tok[0:CH, 4 * i + g, :, :].rearrange("p s c -> p (s c)"), ident[0:CH, 0:CH])
                    last.then_inc(filled, 1)

            def do_wt():
                pe.wait_ge(tables_ready, 1)
                for ri in range(2):
                    for i in range(4):
                        b = enter(("wt", ri, i))
                        for g in range(4):
                            last = tr(b[:, 128 * g:128 * g + 128], AB[:, ri, 4 * i + g, :, :].rearrange("p s c -> p (s c)"), ident)
                        last.then_inc(filled, 1)

            def do_k():
                for par in range(2):
                    rows = slice(64 * par, 64 * par + 64)
                    for i in range(4):
                        b = enter(("k", par, i))
                        for g in range(4):
                            for ri in range(2):
                                last = mm(b[0:GC, 128 * g:128 * g + 128], Bb[rows, ri, 4 * i + g, :],
                                          CA[rows, ri, 4 * i + g, 0:STEP, :].rearrange("p j c -> p (j c)"), start=ri == 0, stop=ri == 1)
                        last.then_inc(filled, 1)

            def do_ws():
                for j in (2, 3):
                    after(("wt", 1, j))
                after(("uc", 7))
                for ri in range(2):
                    for i in range(4):
                        b = enter(("ws", ri, i))
                        for g in range(4):
                            for par in range(2):
                                last = mm(b[64 * par:64 * par + 64, CH * g:CH * g + CH], Wm[:, ri, 4 * i + g, 64 * par:64 * par + 64],
                                          U[:, 2 * (4 * i + g) + par, :], start=True, stop=True)
                        last.then_inc(filled, 1)

            def do_y(par):
                pe.wait_ge(toep_in, 16 * STEP)
                pe.wait_ge(states_ready, 1)
                pe.wait_ge(later_states, 1)
                rows = slice(64 * par, 64 * par + 64)
                for i in range(4):
                    b = enter(("y", par, i))
                    for g in range(4):
                        gp = 4 * i + g
                        o = b[0:CH, 128 * g:128 * g + 128]
                        mm(o, U[:, 2 * gp + par, :], Tm[:, 2 * gp + par, :], start=True, stop=False)
                        for ri in range(2):
                            last = mm(o, H[rows, ri, gp, 0:CH], CA[rows, ri, gp, 1:9, :].rearrange("p j c -> p (j c)"),
                                      start=False, stop=ri == 1)
                    last.then_inc(filled, 1)

            def do_ht():
                after(("y", 1, 3))
                for m in range(4):
                    for hf in range(2):
                        b = enter(("ht", m, hf))
                        for i in range(4):
                            last = tr(b[:, CH * i:CH * i + CH], y_tok[0:CH, 4 * hf + i, 8 * m:8 * m + 8, :].rearrange("p g c -> p (g c)"),
                                      ident[0:CH, 0:CH])
                        last.then_inc(filled, 1)

            def do_qkv(t):
                t0, tn = TILES[t]
                for what, n in (("q", 512), ("kv", 256)):
                    b = enter((what, t))
                    kp = 1024 // n
                    for k in range(KT):
                        w = arrived(group(t), what, k // kp).rearrange("p (k n) -> p k n", n=n)
                        last = mm(b[0:tn, 0:n], xT[:, k, t0:t0 + tn], w[:, k % kp, :], start=k == 0, stop=k == KT - 1)
                    last.then_inc(filled, 1)

            def do_turn(t):
                tn = TILES[t][1]
                pe.wait_ge(roped, plan.index[("qkv", t)])
                b = enter(("qt", t))
                for i in range(4):
                    last = tr(b[:, 128 * i:128 * i + tn], zt[t][0:tn, 128 * i:128 * i + 128], ident[0:tn, 0:tn])
                last.then_inc(filled, 1)
                b = enter(("kt", t))
                tr(b[:, 0:tn], zt[t][0:tn, 512:640], ident[0:tn, 0:tn]).then_inc(filled, 1)

            def do_ss():
                after(("kt", 0))
                pe.wait_ge(caches_in, 32)
                for kv in range(2):
                    rows = slice(64 * kv, 64 * kv + 64)
                    for hf in range(2):
                        b = enter(("ss", kv, hf))
                        for i in range(4):
                            q = qs[rows, 4 * hf + i, :]
                            mm(b[32 * i:32 * i + 32, 0:WIN], q, kc[rows, 4 * hf + i, :], start=True, stop=True)
                            last = mm(b[32 * i:32 * i + 32, WIN:WIN + 64], q, kT[rows, 0:64], start=True, stop=True)
                        last.then_inc(filled, 1)

            def do_pvs():
                PT = PTg[0]
                pe.wait_ge(probs, 1)
                b = enter(("spc",))
                for i in range(4):
                    last = tr(b[:, 128 * i:128 * i + 128], Psm[:, i, 0:WIN], ident)
                last.then_inc(filled, 1)
                b = enter(("spn",))
                for i in range(4):
                    last = tr(b[0:64, 128 * i:128 * i + 128], Psm[:, i, WIN:WIN + 64], ident)
                last.then_inc(filled, 1)
                b = enter(("so",))
                after(("spn",))
                for kv in range(2):
                    for i in range(NSEQ):
                        o = b[64 * kv:64 * kv + 64, 32 * i:32 * i + 32]
                        cols = slice(32 * (i % 4), 32 * (i % 4) + 32)
                        mm(o, vc[:, i, 64 * kv:64 * kv + 64], PT[:, 0, 2 * kv + i // 4, cols], start=True, stop=False)
                        last = mm(o, zt[0][0:64, 640 + 64 * kv:704 + 64 * kv], PT[0:64, 1, 2 * kv + i // 4, cols], start=False, stop=True)
                last.then_inc(filled, 1)

            def do_s(j, kv):
                t = j + 1
                t0, k0, off = TILES[t][0], TILES[t][0] - (128 if j else 0), 0 if j else 128
                after(("kt", 4 if j else 1))
                rows = slice(64 * kv, 64 * kv + 64)
                for hf in range(2):
                    b = enter(("s", j, kv, hf))
                    for i in range(2):
                        last = mm(b[:, 256 * i + off:256 * i + 256], qTg[group(t)][rows, 2 * hf + i, rel(t) - (0 if j else 64):][:, 0:128],
                                  kT[rows, k0:t0 + 128], start=True, stop=True)
                    last.then_inc(filled, 1)

            def do_pv(j, kv):
                P, PT = Pg[group(j + 1)], PTg[group(j + 1)]
                pe.wait_ge(probs, 1 + plan.index[("s", j, kv)])
                for i in range(2):
                    b = enter(("pt", j, kv, i))
                    for e in range(4):
                        last = tr(b[:, 128 * e:128 * e + 128], P[:, 2 * i + e // 2, 128 * (e % 2):128 * (e % 2) + 128], ident)
                    last.then_inc(filled, 1)
                b = enter(("o", j, kv))
                after(("pt", j, kv, 1))
                for hp in range(4):
                    o = b[64 * kv:64 * kv + 64, 128 * hp:128 * hp + 128]
                    for hf in range(0 if j else 1, 2):
                        last = mm(o, zt[j + hf][:, 640 + 64 * kv:704 + 64 * kv],
                                  PT[:, hp // 2, 2 * (hp % 2) + hf, :], start=hf == (0 if j else 1), stop=hf == 1)
                last.then_inc(filled, 1)

            def rows_of(what, g, m):
                c0, cn = COLS[g]
                src, k0, kn = {"gs": (xT, 0, 8), "ga": (xT, 0, 8), "gb": (hgT, 4, 4), "gl": (hgT, 0, 4), "up": (oTg[g], 4 * (m % 2), 4)}[what]
                s0 = 0 if what == "up" else c0
                b = enter((what, g, m))
                w = (arrived(g, "up", m // 2) if what == "up" else arrived(g, "glu", m) if what in ("gb", "gl")
                     else arrived(g, what, m)).rearrange("p (k n) -> p k n", k=8)
                for k in range(kn):
                    last = mm(b[:, 0:cn], w[:, k0 + k, :], src[:, k, s0:s0 + cn], start=k == 0, stop=k == kn - 1)
                last.then_inc(filled, 1)

            def do_gates(g, m):
                rows_of("gs", g, m)
                rows_of("ga", g, m)

            def do_merge(g, m):
                if m == 0:
                    after(("o", 3 if g else 0, 1))
                    after(("ht", 3, 1))
                for what in ("gb", "gl", "up"):
                    rows_of(what, g, m)

            def do_wo(t):
                g, tn = group(t), TILES[t][1]
                after(("up", g, 7))
                for hf in range(2):
                    b = enter(("wo", t, hf))
                    for k in range(KT):
                        w = arrived(g, "wo", k)
                        last = mm(b[0:tn, :], mTg[g][:, k, rel(t):rel(t) + tn], w[:, 512 * hf:512 * hf + 512], start=k == 0, stop=k == KT - 1)
                    last.then_inc(filled, 1)

            def do_xt(t):
                tn = TILES[t][1]
                pe.wait_ge(x1_s, plan.index[("wo", t)])
                for hf in range(2):
                    b = enter(("xt", t, hf))
                    for i in range(4):
                        k = 4 * hf + i
                        last = tr(b[:, 128 * i:128 * i + tn], x1[t][0:tn, 128 * k:128 * k + 128], ident[0:tn, 0:tn])
                    last.then_inc(filled, 1)

            def do_wq(g, h):
                c0, cn = COLS[g]
                after(("xt", GROUPS[g][-1], 1))
                b = enter(("wq", g, h))
                w = arrived(g, "wq", h).rearrange("p (k n) -> p k n", k=8)
                for k in range(KT):
                    last = mm(b[:, 0:cn], w[:, k, :], xT[:, k, c0:c0 + cn], start=k == 0, stop=k == KT - 1)
                last.then_inc(filled, 1)

            def do_sc(t, i):
                g, tn = group(t), TILES[t][1]
                after(("wq", g, 4 * i + 2))
                after(("wq", g, 4 * i + 3))
                k12 = s("k12", NH, KEYS)
                for side in range(2):
                    rows = slice(64 * side, 64 * side + 64)
                    b = enter(("sc", t, side, i))
                    for h in range(4):
                        last = mm(b[0:tn, 128 * h:128 * h + 128], q2T(t, 4 * i + h)[rows], k12[rows, 4 * i + h, :],
                                  start=True, stop=True)
                    last.then_inc(filled, 1)

            def weigh(t, c):
                tn, ns, base = TILES[t][1], n_slots(t), slot_base[t]
                for k in range(STEP_SLOTS * c, STEP_SLOTS * c + STEP_SLOTS):
                    q = base + k
                    if k == 0:
                        enter(("po", t, 0)), enter(("po", t, 1))
                    if on_dve[q]:
                        continue
                    d = q - by_dve[q]
                    pe.wait_ge(diag_s, d + 1)
                    pe.wait_ge(g_v[v_at.place[q]], 16 * v_at.nth[q])
                    for hf in range(2):
                        last = mm(bank[6 + hf][0:tn, :], diag[:, d % DIAGS, 0:tn], ring_v[v_at.place[q]][:, 512 * hf:512 * hf + 512],
                                  start=k == 0, stop=t not in V_SHARE and k == ns - 1)
                    last.then_inc(v_used, 1)
                if c == ns // STEP_SLOTS - 1 and t < 2:
                    pe.wait_ge(v_used_d, by_dve[base + ns - 1])
                    for hf in range(2):
                        last = mm(bank[6 + hf][0:tn, :], s("fold") if t == 0 else ident, acc[:, 512 * hf:512 * hf + 512],
                                  start=False, stop=True)
                    last.then_inc(v_used, 1)

            def do_peer(t, c):
                if c:
                    weigh(t, c - 1)

            def do_last(t):
                weigh(t, n_slots(t) // STEP_SLOTS - 1)

            here = {"u": do_u, "ut": do_ut, "uc": do_uc, "wt": do_wt, "k": do_k, "ws": do_ws, "y": do_y, "ht": do_ht, "qkv": do_qkv,
                    "turn": do_turn, "ss": do_ss, "pvs": do_pvs, "s": do_s, "pv": do_pv, "gates": do_gates, "merge": do_merge,
                    "wo": do_wo, "xt": do_xt, "wq": do_wq, "sc": do_sc, "peer": do_peer, "last": do_last}
            for item in mixer_first(plan.items):
                if item[0] in here:
                    here[item[0]](*item[1:])

        @block.vector
        def _(dve):
            V = nc.vector
            steps = [0]

            def step(ins):
                steps[0] += 1
                ins.then_inc(vstep, 1)
                dve.wait_ge(vstep, steps[0])

            def drain(key, ins):
                who, n = plan.drained[key]
                ins.then_inc(drained[who], 1)
                dve.wait_ge(drained[who], n)

            def full(key):
                dve.wait_ge(filled, plan.filled[key])
                return bank[plan.bank[key]]

            def cmul(out, x, y, t1, t2):
                n = x.shape[2]
                step(V.tensor_tensor(t1, x, y[:, 0:1, :].broadcast_to([128, 2, n]), ALU.mult))
                step(V.tensor_tensor(t2, x[:, 1::-1, :], y[:, 1:2, :].broadcast_to([128, 2, n]), ALU.mult))
                step(V.tensor_tensor(out[:, 0, :], t1[:, 0, :], t2[:, 0, :], ALU.subtract))
                step(V.tensor_tensor(out[:, 1, :], t1[:, 1, :], t2[:, 1, :], ALU.add))

            ta, tb, w, wk, T, E = (cx[:, i, :, :] for i in range(6))
            a_, num = cx[:, 6, :, :], cx[:, 8, :, :]

            def do_tables():
                dve.wait_ge(tables_in, 16)
                dve.wait_ge(astep, 1)
                step(V.tensor_copy(a_[:, 0, :], s("are")))
                step(V.tensor_copy(a_[:, 1, :], s("aim")))
                step(V.scalar_tensor_tensor(out=w, in0=a_, scalar=1.0 / 256, in1=cx[:, 7, 0:1, :].broadcast_to([128, 2, GP]),
                                            op0=ALU.mult, op1=ALU.mult))
                step(V.tensor_scalar(T, w, 1.0 / 8, None, ALU.mult))
                step(V.tensor_scalar(T[:, 0, :], T[:, 0, :], 1.0, None, ALU.add))
                for k in range(7, 0, -1):
                    step(V.tensor_scalar(wk, w, 1.0 / k, None, ALU.mult))
                    cmul(T, wk, T, ta, tb)
                    if k > 1:
                        step(V.tensor_scalar(T[:, 0, :], T[:, 0, :], 1.0, None, ALU.add))
                step(V.tensor_copy(E, T))
                for _ in range(8):
                    step(V.tensor_copy(wk, E))
                    step(V.tensor_scalar(wk[:, 0, :], wk[:, 0, :], 2.0, None, ALU.add))
                    cmul(E, wk, E, ta, tb)
                step(V.tensor_tensor(ta, a_, a_, ALU.mult))
                step(V.tensor_tensor(tb[:, 0, :], ta[:, 0, :], ta[:, 1, :], ALU.add))
                step(V.reciprocal(tb[:, 1, :], tb[:, 0, :]))
                step(V.tensor_tensor(wk, a_, tb[:, 1:2, :].broadcast_to([128, 2, GP]), ALU.mult))
                step(V.tensor_scalar(wk[:, 1, :], wk[:, 1, :], -1.0, None, ALU.mult))
                cmul(num, E, wk, ta, tb)
                bb, cc = s("bb", 2, GP * GC).rearrange("p a (g c) -> p a g c", c=GC), s("cc", 2, GP * GC).rearrange("p a (g c) -> p a g c", c=GC)
                small1 = T1.rearrange("p a b c -> p (a b c)")[:, 0:256].rearrange("p (g c) -> p g c", c=GC)
                small2 = T2.rearrange("p a b c -> p (a b c)")[:, 0:256].rearrange("p (g c) -> p g c", c=GC)

                def over_c(x):
                    return x.unsqueeze(2).broadcast_to([128, GP, GC])

                step(V.tensor_tensor(small1, bb[:, 0], over_c(num[:, 0, :]), ALU.mult))
                step(V.tensor_tensor(small2, bb[:, 1], over_c(num[:, 1, :]), ALU.mult))
                step(V.tensor_tensor(Bb[:, 0], small1, small2, ALU.subtract))
                step(V.tensor_tensor(small1, bb[:, 0], over_c(num[:, 1, :]), ALU.mult))
                step(V.tensor_tensor(small2, bb[:, 1], over_c(num[:, 0, :]), ALU.mult))
                step(V.tensor_tensor(Bb[:, 1], small1, small2, ALU.add))
                step(V.memset(pw[:, 0, :, 0], 1.0))
                step(V.memset(pw[:, 1, :, 0], 0.0))
                step(V.tensor_scalar(pw[:, 0, :, 1], E[:, 0, :], 1.0, None, ALU.add))
                step(V.tensor_copy(pw[:, 1, :, 1], E[:, 1, :]))
                for j in range(2, 9):
                    cmul(pw[:, :, :, j], pw[:, :, :, j - 1], pw[:, :, :, 1], ta, tb)
                step(V.tensor_copy(a8[:, 0], pw[:, 0:1, :, 8].broadcast_to([128, 2, GP])))
                step(V.tensor_scalar(a8[:, 1, 0, :], pw[:, 1, :, 8], -1.0, None, ALU.mult))
                step(V.tensor_copy(a8[:, 1, 1, :], pw[:, 1, :, 8]))


                def outer(out0, out1, x, powers, hf, n, sign):
                    g = slice(8 * hf, 8 * hf + 8)
                    t1, t2 = T1[:, :, 0:n, :], T2[:, :, 0:n, :]
                    X = [x[:, r, g, :].unsqueeze(2).broadcast_to([128, 8, n, GC]) for r in range(2)]
                    Q = [powers[r][:, g, :].unsqueeze(3).broadcast_to([128, 8, n, GC]) for r in range(2)]
                    step(V.tensor_tensor(t1, X[0], Q[0], ALU.mult))
                    step(V.tensor_tensor(t2, X[1], Q[1], ALU.mult))
                    step(V.tensor_tensor(out0[:, g], t1, t2, ALU.subtract))
                    step(V.tensor_tensor(t1, X[0], Q[1], ALU.mult))
                    step(V.tensor_tensor(t2, X[1], Q[0], ALU.mult))
                    if sign > 0:
                        step(V.tensor_tensor(out1[:, g], t1, t2, ALU.add))
                    else:
                        step(V.tensor_tensor(t1, t1, t2, ALU.add))
                        step(V.tensor_scalar(out1[:, g], t1, -1.0, None, ALU.mult))

                for hf in range(2):
                    outer(CA[:, 0], CA[:, 1], cc, [pw[:, r, :, :] for r in range(2)], hf, 9, -1)
                for hf in range(2):
                    outer(AB[:, 0], AB[:, 1], Bb, [pw[:, r, :, 7::-1] for r in range(2)], hf, 8, 1)
                dve.wait_ge(small_in, 16)
                step(V.tensor_copy(H[:, :, :, 0:NSEQ], s("h0", 2, GP, NSEQ)))
                V.memset(H[:, :, :, NSEQ:NSEQ + 1], 0.0).then_inc(tables_ready, 1)
                dve.wait_ge(tables_ready, 1)

            def do_wt():
                for ri in range(2):
                    for i in (1, 3):
                        b = full(("wt", ri, i))
                        drain(("wt", ri, i), V.tensor_copy(Wm[:, ri, 4 * i:4 * i + 4, :].rearrange("p g n -> p (g n)"), b[:, :]))

            def do_k():
                wait_item(dve, ("uc",))
                for par in range(2):
                    for i in (1, 3):
                        b = full(("k", par, i))
                        drain(("k", par, i), V.tensor_copy(Kt[0:GC, 8 * i + par:8 * i + par + 7:2, :, :].rearrange("p g j c -> p g (j c)"),
                                                           b[0:GC, :].rearrange("p (g n) -> p g n", g=4)))
                dve.wait_ge(drained["A"], plan.drained[("k", 1, 2)][1])
                step(V.tensor_tensor(eye_d[0:GC], s("dskip", G, GC)[0:GC], ident[0:GC, 0:GC].unsqueeze(1).broadcast_to([GC, G, GC]), ALU.mult))
                V.tensor_tensor(Kt[0:GC, :, 0, :], Kt[0:GC, :, 0, :], eye_d[0:GC], ALU.add).then_inc(kernel_ready, 1)

            def do_ws():
                for ri in range(2):
                    for i in (1, 3):
                        b = full(("ws", ri, i))
                        drain(("ws", ri, i), V.tensor_copy(Wst[:, ri, 4 * i:4 * i + 4, :].rearrange("p g n -> p (g n)"), b[:, 0:4 * CH]))

            def do_rec():
                dve.wait_ge(drained["A"], plan.drained[("ws", 1, 2)][1])
                for c in range(NSEQ, FIRST):
                    step(V.tensor_tensor(ta, H[:, :, :, c], a8[:, 0], ALU.mult))
                    step(V.tensor_tensor(tb, H[:, 1::-1, :, c], a8[:, 1], ALU.mult))
                    step(V.tensor_tensor(ta, ta, Wst[:, :, :, c], ALU.add))
                    ins = V.tensor_tensor(H[:, :, :, c + 1], ta, tb, ALU.add)
                    if c < FIRST - 1:
                        step(ins)
                    else:
                        ins.then_inc(states_ready, 1)

            rope = s("rope", 5, 2, 8)

            def do_qkv(t):
                tn, z = TILES[t][1], zt[t]
                if t == 2:
                    wait_item(dve, ("ht",))
                b = full(("q", t))
                drain(("q", t), V.tensor_tensor(z[0:tn, 0:512], b[0:tn, :], s("bqkv")[0:tn, 0:512], ALU.add))
                b = full(("kv", t))
                drain(("kv", t), V.tensor_tensor(z[0:tn, 512:768], b[0:tn, 0:256], s("bqkv")[0:tn, 512:768], ALU.add))
                hd = z[0:tn, 0:640].rearrange("p (h d) -> p h d", d=HD)
                lo, hi = hd[:, :, 0:8], hd[:, :, 8:16]
                cos, sin = (rope[0:tn, t, r, :].unsqueeze(1).broadcast_to([tn, 10, 8]) for r in range(2))
                step(V.tensor_tensor(rt[0:tn, 0], lo, cos, ALU.mult))
                step(V.tensor_tensor(rt[0:tn, 1], hi, sin, ALU.mult))
                step(V.tensor_tensor(rt[0:tn, 2], hi, cos, ALU.mult))
                step(V.tensor_tensor(rt[0:tn, 3], lo, sin, ALU.mult))
                step(V.tensor_tensor(lo, rt[0:tn, 0], rt[0:tn, 1], ALU.subtract))
                V.tensor_tensor(hi, rt[0:tn, 2], rt[0:tn, 3], ALU.add).then_inc(roped, 1)
                dve.wait_ge(roped, plan.index[("qkv", t)])

            def softmax(n, scores, sink, width, st):
                mx, ex, sm, rs = (stat[:, 8 * i:8 * i + width] for i in range(4))
                step(V.tensor_reduce(mx, scores, AX, ALU.max))
                step(V.tensor_tensor(mx, mx, sink, ALU.max))
                step(V.tensor_tensor(ex, sink, mx, ALU.subtract))
                V.tensor_tensor(scores, scores, mx.unsqueeze(2).broadcast_to([128, width, st]), ALU.subtract).then_inc(scored, 1)
                dve.wait_ge(expd_s, n)
                step(V.tensor_reduce(sm, scores, AX, ALU.add))
                step(V.tensor_tensor(sm, sm, ex, ALU.add))
                step(V.reciprocal(rs, sm))
                V.tensor_tensor(scores, scores, rs.unsqueeze(2).broadcast_to([128, width, st]), ALU.mult).then_inc(probs, 1)
                dve.wait_ge(probs, n)

            masks, maskp = s("masks", 2, WIN + 64), s("maskp")

            def do_ss():
                for kv in range(2):
                    for hf in range(2):
                        b = full(("ss", kv, hf))
                        drain(("ss", kv, hf), V.scalar_tensor_tensor(out=Psm[:, 2 * kv + hf, :], in0=b[:, 0:WIN + 64], scalar=HD ** -0.5,
                                                                     in1=masks[:, hf, :], op0=ALU.mult, op1=ALU.add))
                sk = stat[:, 60:64]
                step(V.tensor_copy(sk.rearrange("p (a b) -> p a b", a=2), s("sinks").unsqueeze(2).broadcast_to([128, 2, 2])))
                softmax(1, Psm, sk, 4, WIN + 64)

            def do_pvs():
                b = full(("so",))
                for kv in range(2):
                    rows = slice(64 * kv, 64 * kv + 64)
                    ins = V.tensor_copy(oTg[0][rows, :, 0:64].rearrange("p h (b q) -> p b h q", q=8),
                                        b[rows, 0:256].rearrange("p (b h q) -> p b h q", b=8, h=4))
                    step(ins) if kv == 0 else drain(("so",), ins)

            def do_s(j, kv):
                n, P = plan.index[("s", j, kv)], Pg[group(j + 1)]
                for hf in range(2):
                    b = full(("s", j, kv, hf))
                    if hf == 0:
                        prev = plan.items[:plan.items.index(("s", j, kv))]
                        dve.wait_ge(filled, max(plan.filled[k] for k in (("spn",), *[("pt", *i[1:], 1) for i in prev if i[0] == "pv"])))
                    o = P[:, 2 * hf:2 * hf + 2, :]
                    if j == 0:
                        step(V.memset(o[:, :, 0:128], NEG))
                        drain(("s", j, kv, hf), V.scalar_tensor_tensor(
                            out=o[:, :, 128:256], in0=b[:, :].rearrange("p (a n) -> p a n", a=2)[:, :, 128:256], scalar=HD ** -0.5,
                            in1=maskp[:, 128:256].unsqueeze(1).broadcast_to([128, 2, 128]), op0=ALU.mult, op1=ALU.add))
                    else:
                        drain(("s", j, kv, hf), V.scalar_tensor_tensor(
                            out=o, in0=b[:, :].rearrange("p (a n) -> p a n", a=2), scalar=HD ** -0.5,
                            in1=maskp.unsqueeze(1).broadcast_to([128, 2, 256]), op0=ALU.mult, op1=ALU.add))
                softmax(1 + n, P, s("sinkp")[:, 4 * kv:4 * kv + 4], 4, 2 * WIN)

            def do_pv(j, kv):
                t = j + 1
                c, rows = rel(t), slice(64 * kv, 64 * kv + 64)
                b = full(("o", j, kv))
                drain(("o", j, kv), V.tensor_copy(oTg[group(t)][rows, :, c:c + 128], b[rows, :].rearrange("p (h n) -> p h n", h=4)))

            def do_merge(g, m):
                cn = COLS[g][1]
                if g and m == 0:
                    wait_item(dve, ("pv", 3, 1))
                    dve.wait_ge(kv_out, 64)
                gt, q = gateg[g][:, m % 2, :, :], partg[g]
                s_gate, a_gate = (gt[:, 0], gt[:, 1]) if g else (sg[:, 0, m], sg[:, 1, m])
                b = full(("gl", g, m))
                dve.wait_ge(drained["A"], plan.drained[("gb", g, m)][1])
                drain(("gl", g, m), V.scalar_tensor_tensor(out=q[:, 0], in0=b[:, 0:cn], scalar=s("bglu")[:, m:m + 1], in1=gt[:, 2 if g else 0],
                                                           op0=ALU.add, op1=ALU.mult))
                step(V.tensor_tensor(q[:, 0], q[:, 0], s_gate, ALU.mult))
                b = full(("up", g, m))
                step(V.tensor_tensor(q[:, 1], b[:, 0:cn], a_gate, ALU.mult))
                drain(("up", g, m), V.tensor_tensor(mTg[g][:, m, :], q[:, 0], q[:, 1], ALU.add))

            norms = [0]

            def layer_norm(out, r, tn, ln):
                norms[0] += 1
                st, mv = stat[0:tn, 64:76], stat[0:tn, 76:78]
                for hf in range(2):
                    step(V.bn_stats(st[:, 6 * hf:6 * hf + 6], r[:, 512 * hf:512 * hf + 512]))
                step(V.bn_aggr(mv, st))
                V.tensor_scalar(stat[0:tn, 78:79], mv[:, 1:2], EPS, None, ALU.add).then_inc(var_s, 1)
                dve.wait_ge(std_s, norms[0])
                step(V.reciprocal(stat[0:tn, 78:79], stat[0:tn, 79:80]))
                step(V.tensor_scalar(r, r, mv[:, 0:1], stat[0:tn, 78:79], ALU.subtract, ALU.mult))
                step(V.tensor_tensor(r, r, ln[0:tn, 0, :], ALU.mult))
                return V.tensor_tensor(out, r, ln[0:tn, 1, :], ALU.add)

            def do_wo(t):
                tn = TILES[t][1]
                dve.wait_ge(x2_in if t > 1 else x_in, 16 * len(GROUPS[group(t)]))
                dve.wait_ge(ln_in, 16)
                for hf in range(2):
                    b = full(("wo", t, hf))
                    half = slice(512 * hf, 512 * hf + 512)
                    drain(("wo", t, hf), V.scalar_tensor_tensor(out=x1[t][0:tn, half], in0=x1[t][0:tn, half], scalar=ALPHA,
                                                                in1=b[0:tn, :], op0=ALU.mult, op1=ALU.add))
                layer_norm(x1[t][0:tn, :], x1[t][0:tn, :], tn, ln1).then_inc(x1_s, 1)
                dve.wait_ge(x1_s, plan.index[("wo", t)])

            def do_wq(g, h):
                if g and h % 2:
                    b = full(("wq", g, h))
                    drain(("wq", g, h), V.tensor_copy(q2B[:, h, :], b[:, 0:COLS[g][1]]))

            def top_keys(t, h):
                tn = TILES[t][1]
                for side in range(2):
                    b = full(("sc", t, side, h // 4))
                    sc = b[0:tn, 128 * (h % 4):128 * (h % 4) + 128]
                    va, vb = v16[0:tn, side, h, 0:8], v16[0:tn, side, h, 8:16]
                    ia, ib = i16[0:tn, side, h, 0:8], i16[0:tn, side, h, 8:16]
                    rest = scr[0:tn, 0:128]
                    step(V.max(out=va, in_=sc))
                    step(V.max_index(out=ia, in_max=va, in_values=sc))
                    ins = V.match_replace(out=rest, in_to_replace=va, in_values=sc, imm_value=-3.0e38)
                    drain(("sc", t, side, h // 4), ins) if h % 4 == 3 else step(ins)
                    step(V.max(out=vb, in_=rest))
                    step(V.max_index(out=ib, in_max=vb, in_values=rest))
                cd = cand[0:tn].rearrange("p a b -> p (a b)")
                step(V.tensor_tensor(cand[0:tn], v16[0:tn, 0, h, :].unsqueeze(2).broadcast_to([tn, TOPK, TOPK]),
                                     v16[0:tn, 1, h, :].unsqueeze(1).broadcast_to([tn, TOPK, TOPK]), ALU.add))
                rest = scr[0:tn, 0:256]
                step(V.max(out=top[0:tn, h, 0:8], in_=cd))
                step(V.max_index(out=pos[0:tn, h, 0:8], in_max=top[0:tn, h, 0:8], in_values=cd))
                step(V.match_replace(out=rest, in_to_replace=top[0:tn, h, 0:8], in_values=cd, imm_value=-3.0e38))
                step(V.max(out=top[0:tn, h, 8:16], in_=rest))
                step(V.max_index(out=pos[0:tn, h, 8:16], in_max=top[0:tn, h, 8:16], in_values=rest))

            def do_choose(t, part):
                n, tn = ORDER.index(t), TILES[t][1]
                heads, half = slice(4 * part, 4 * part + 4), slice(64 * part, 64 * part + 64)
                gt = gts[0:tn, n % 2, half].rearrange("p (h k) -> p h k", h=NH // 2)
                p64 = pos[0:tn, heads].rearrange("p h k -> p (h k)")
                V.tensor_tensor(gt, top[0:tn, heads], top[0:tn, heads, 0:1].broadcast_to([tn, NH // 2, TOPK]), ALU.subtract).then_inc(sc_s, 1)
                step(V.tensor_scalar(pos2[0:tn, 0, half], p64, 4, None, ALU.logical_shift_right))
                step(V.tensor_scalar(pos2[0:tn, 1, half], p64, 15, None, ALU.bitwise_and))
                step(V.tensor_copy(posf[0:tn, :, half], pos2[0:tn, :, half]))
                step(V.tensor_copy(i16f[0:tn, :, heads], i16[0:tn, :, heads]))
                for side in range(2):
                    of_heads = eq[0:tn].rearrange("p (h k) a -> p h k a", h=NH // 2)
                    step(V.tensor_tensor(eq[0:tn], posf[0:tn, side, half].unsqueeze(2).broadcast_to([tn, 64, TOPK]),
                                         s("iota")[0:tn].unsqueeze(1).broadcast_to([tn, 64, TOPK]), ALU.is_equal))
                    step(V.tensor_tensor(of_heads, of_heads, i16f[0:tn, side, heads].unsqueeze(2).broadcast_to(
                                         [tn, NH // 2, TOPK, TOPK]), ALU.mult))
                    step(V.tensor_reduce(ef[0:tn, side, half], eq[0:tn], AX, ALU.add))
                step(V.scalar_tensor_tensor(out=ef[0:tn, 0, half], in0=ef[0:tn, 0, half], scalar=float(KEYS), in1=ef[0:tn, 1, half],
                                            op0=ALU.mult, op1=ALU.add))
                step(V.tensor_copy(idx[0:tn, n % 2, half], ef[0:tn, 0, half]))
                dve.wait_ge(sce_s, 2 * n + part + 1)
                sm, rs = stat[0:tn, 20:24], stat[0:tn, 28:32]
                step(V.tensor_reduce(sm, gt, AX, ALU.add))
                step(V.reciprocal(rs, sm))
                V.tensor_tensor(gt, gt, rs.unsqueeze(2).broadcast_to([tn, NH // 2, TOPK]), ALU.mult).then_inc(idx_s, 1)
                dve.wait_ge(idx_s, 2 * n + part + 1)

            def do_top(t, h):
                top_keys(t, h)

            done = [0]

            def gated(t, c):
                n = ORDER.index(t)
                gt = gtf if t == 0 else gts[:, n % 2, :]
                done[0] += 1
                dve.wait_ge(act_s, done[0])
                k = slice(STEP_SLOTS * c, STEP_SLOTS * c + STEP_SLOTS)
                V.tensor_tensor(aact[:, n % 2, k], hact[:, n % 2, k], gt[:, k], ALU.mult).then_inc(a_s, 1)

            def add_row(t, k):
                n, q = ORDER.index(t), slot_base[t] + k
                if not on_dve[q]:
                    return
                dve.wait_ge(a_s, done[0])
                dve.wait_ge(g_v[v_at.place[q]], 16 * v_at.nth[q])
                if not any(on_dve[slot_base[t]:q]):
                    if n:
                        dve.wait_ge(v_used, by_pe[slot_base[t] - 1] + 1)
                    V.tensor_scalar(acc, ring_v[v_at.place[q]], aact[:, n % 2, k:k + 1], None, ALU.mult).then_inc(v_used_d, 1)
                else:
                    dve.wait_ge(v_used_d, by_dve[q] - 1)
                    V.scalar_tensor_tensor(out=acc, in0=ring_v[v_at.place[q]], scalar=aact[:, n % 2, k:k + 1], in1=acc,
                                           op0=ALU.mult, op1=ALU.add).then_inc(v_used_d, 1)

            def do_peer(t, c):
                n, base = ORDER.index(t), slot_base[t]
                if t == 0 and c == 0:
                    dve.wait_ge(fold_in, 16 * 5)
                for k in range(STEP_SLOTS * c, STEP_SLOTS * c + STEP_SLOTS):
                    q = base + k
                    dve.wait_ge(g_u[u_at.place[q]], 16 * u_at.nth[q])
                    V.tensor_tensor_reduce(out=ring_u[u_at.place[q]], in0=ring_u[u_at.place[q]], in1=x1[t], scale=1.0, scalar=0.0,
                                           op0=ALU.mult, op1=ALU.add, accum_out=hdot[:, n % 2, k:k + 1]).then_inc(dots, 1)
                    if c:
                        if k == STEP_SLOTS * c:
                            gated(t, c - 1)
                        add_row(t, k - STEP_SLOTS)

            def do_last(t):
                gated(t, n_slots(t) // STEP_SLOTS - 1)
                for k in range(n_slots(t) - STEP_SLOTS, n_slots(t)):
                    add_row(t, k)

            def do_final(t):
                tn = TILES[t][1]
                dve.wait_ge(v_used, by_pe[slot_base[t] + n_slots(t) - 1] + (t < 2))
                dve.wait_ge(ln2_in, 16)
                for hf in range(2):
                    half = slice(512 * hf, 512 * hf + 512)
                    drain(("po", t, hf), V.scalar_tensor_tensor(out=x1[t][0:tn, half], in0=x1[t][0:tn, half], scalar=ALPHA,
                                                                in1=bank[6 + hf][0:tn, :], op0=ALU.mult, op1=ALU.add))
                layer_norm(x1[t][0:tn, :], x1[t][0:tn, :], tn, ln2).then_inc(y_s, 1)

            here = {"tables": do_tables, "wt": do_wt, "k": do_k, "ws": do_ws, "rec": do_rec, "qkv": do_qkv, "ss": do_ss, "pvs": do_pvs,
                    "s": do_s, "pv": do_pv, "merge": do_merge, "wo": do_wo, "wq": do_wq, "top": do_top, "choose": do_choose,
                    "peer": do_peer, "last": do_last, "final": do_final}
            for item in plan.items:
                if item[0] in here:
                    here[item[0]](*item[1:])

        @block.scalar
        def _(act):
            S = nc.scalar
            steps = [0]

            def step(ins):
                steps[0] += 1
                ins.then_inc(astep, 1)
                act.wait_ge(astep, steps[0])

            def drain(key, ins):
                who, n = plan.drained[key]
                ins.then_inc(drained["A"], 1)
                act.wait_ge(drained["A"], n)

            def full(key):
                act.wait_ge(filled, plan.filled[key])
                return bank[plan.bank[key]]

            def copy(out, in_):
                return S.activation(out, in_, ACT.Copy)

            def do_tables():
                cut = SM["cc"][1]
                act.dma_start(small[:, 0:cut], io["small"][:, 0:cut]).then_inc(tables_in, 16)
                act.dma_start(small[:, cut:SMC], io["small"][:, cut:SMC]).then_inc(small_in, 16)
                act.wait_ge(tables_in, 16)
                step(S.activation(cx[:, 7, 0, :], s("ldt"), ACT.Exp))

            def do_u():
                for c, (c0, cn) in enumerate(COLS):
                    for m in range(4):
                        b = full(("u", c, m))
                        drain(("u", c, m), S.activation(uT[:, m, c0:c0 + cn], b[:, 0:cn], ACT.Identity, bias=s("bu")[:, m:m + 1]))

            def do_ut():
                act.wait_ge(small_in, 16)
                for i in range(8):
                    b = full(("ut", i))
                    drain(("ut", i), copy(u_tok[0:CH, :, i, :], b[0:CH, :].rearrange("p (g c) -> p g c", c=GC)))

            def do_uc():
                for i in range(8):
                    b = full(("uc", i))
                    drain(("uc", i), copy(U[:, 4 * i:4 * i + 4, :].rearrange("p g n -> p (g n)"), b[:, 0:4 * CH]))

            def do_wt():
                for ri in range(2):
                    for i in (0, 2):
                        b = full(("wt", ri, i))
                        drain(("wt", ri, i), copy(Wm[:, ri, 4 * i:4 * i + 4, :].rearrange("p g n -> p (g n)"), b[:, :]))

            def do_k():
                for par in range(2):
                    for i in (0, 2):
                        b = full(("k", par, i))
                        drain(("k", par, i), copy(Kt[0:GC, 8 * i + par:8 * i + par + 7:2, :, :].rearrange("p g j c -> p g (j c)"),
                                                  b[0:GC, :].rearrange("p (g n) -> p g n", g=4)))

            def do_ws():
                for ri in range(2):
                    for i in (0, 2):
                        b = full(("ws", ri, i))
                        drain(("ws", ri, i), copy(Wst[:, ri, 4 * i:4 * i + 4, :].rearrange("p g n -> p (g n)"), b[:, 0:4 * CH]))

            def do_y(par):
                act.wait_ge(toep_in, 16 * STEP)
                for i in range(4):
                    b = full(("y", par, i))
                    drain(("y", par, i), S.activation(y_tok[0:CH, :, 8 * i + par:8 * i + par + 7:2, :].rearrange("p j g c -> p g j c"),
                                                      b[0:CH, :].rearrange("p (g j c) -> p g j c", g=4, j=STEP), ACT.Gelu))

            def do_ht():
                wait_item(act, ("pv", 0, 1))
                act.wait_ge(kv_out, 32)
                hg_view = hgT[:, :, :].rearrange("p m (n t) -> p m t n", t=STEP)
                for m in range(4):
                    for hf in range(2):
                        b = full(("ht", m, hf))
                        drain(("ht", m, hf), copy(hg_view[:, m, 4 * hf:4 * hf + 4, :], b[:, 0:4 * CH].rearrange("p (t n) -> p t n", t=4)))

            def do_turn(t):
                t0, tn = TILES[t]
                b = full(("qt", t))
                if t == 0:
                    drain(("qt", t), copy(qs.rearrange("p b (h q) -> p h b q", h=HP),
                                          b[:, :].rearrange("p (h n) -> p h n", h=4)[:, :, 0:tn].rearrange("p h (b q) -> p h b q", q=STEP)))
                else:
                    c = 0 if t == 1 else rel(t)
                    drain(("qt", t), copy(qTg[group(t)][:, :, c:c + 128], b[:, :].rearrange("p (h n) -> p h n", h=4)))
                b = full(("kt", t))
                drain(("kt", t), copy(kT[:, t0:t0 + tn], b[:, 0:tn]))
                if t == 4:
                    act.wait_ge(roped, plan.index[("qkv", t)])
                    act.dma_start(io["kwp"], zt[4][:, 512:640]).then_inc(kv_out, 16)
                    act.dma_start(io["vwp"], zt[4][:, 640:768]).then_inc(kv_out, 16)
                if t == 0:
                    act.wait_ge(roped, plan.index[("qkv", t)])
                    for o, c in (("kws", 512), ("vws", 640)):
                        act.dma_start(io[o][:, WIN - STEP:WIN, :], zt[0][0:64, c:c + 128]).then_inc(kv_out, 16)

            def exponentials(n, scores, width):
                act.wait_ge(scored, n)
                step(S.activation(stat[:, 8:8 + width], stat[:, 8:8 + width], ACT.Exp))
                S.activation(scores, scores, ACT.Exp).then_inc(expd_s, 1)

            def do_ss():
                exponentials(1, Psm, 4)

            def do_pvs():
                PT = PTg[0]
                b = full(("spc",))
                drain(("spc",), copy(PT[:, 0].rearrange("p a b -> p (a b)"), b[:, :]))
                b = full(("spn",))
                drain(("spn",), copy(PT[0:64, 1].rearrange("p a b -> p (a b)"), b[0:64, :]))

            def do_s(j, kv):
                exponentials(1 + plan.index[("s", j, kv)], Pg[group(j + 1)], 4)

            def do_pv(j, kv):
                n, PT = plan.items.index(("pv", j, kv)), PTg[group(j + 1)]
                act.wait_ge(filled, max(plan.filled[k] for k in (("so",), *[("o", *i[1:]) for i in plan.items[:n] if i[0] == "pv"])))
                for i in range(2):
                    b = full(("pt", j, kv, i))
                    drain(("pt", j, kv, i), copy(PT[:, i].rearrange("p a b -> p (a b)"), b[:, :]))

            def do_gates(g, m):
                if m == 0:
                    wait_item(act, ("pv", 3, 1) if g else ("ws",))
                    if g:
                        act.wait_ge(kv_out, 64)
                if g and m >= 2:
                    act.wait_ge(drained["D"], plan.drained[("up", g, m - 2)][1])
                for i, what in enumerate(("gs", "ga")):
                    b = full((what, g, m))
                    drain((what, g, m), S.activation(gateg[1][:, m % 2, i] if g else sg[:, i, m], b[:, 0:COLS[g][1]], ACT.Sigmoid,
                                                     bias=s("b" + what)[:, m:m + 1]))

            def do_merge(g, m):
                if g == 0 and m == 0:
                    wait_item(act, ("pv", 0, 1))
                if g == 0 and m >= 2:
                    act.wait_ge(drained["D"], plan.drained[("up", g, m - 2)][1])
                b = full(("gb", g, m))
                drain(("gb", g, m), S.activation(gateg[g][:, m % 2, 2 if g else 0], b[:, 0:COLS[g][1]], ACT.Sigmoid,
                                                 bias=s("bglu")[:, 8 + m:9 + m]))

            norms = [0]

            def deviation(tn):
                norms[0] += 1
                act.wait_ge(var_s, norms[0])
                S.activation(stat[0:tn, 79:80], stat[0:tn, 78:79], ACT.Sqrt).then_inc(std_s, 1)

            def do_wo(t):
                deviation(TILES[t][1])

            def do_xt(t):
                t0, tn = TILES[t]
                for hf in range(2):
                    b = full(("xt", t, hf))
                    drain(("xt", t, hf), copy(xT[:, 4 * hf:4 * hf + 4, t0:t0 + tn], b[:, :].rearrange("p (k n) -> p k n", k=4)[:, :, 0:tn]))

            def do_wq(g, h):
                if h % 2 == 0 or g == 0:
                    if h == 0:
                        wait_item(act, ("wo", GROUPS[g][-1]))
                    b = full(("wq", g, h))
                    if g == 0:
                        step(copy(q2T(0, h), b[:, 0:64]))
                    drain(("wq", g, h), copy(q2B[:, h, :] if g else q2T(1, h), b[:, 0:COLS[g][1]] if g else b[:, 64:192]))

            def do_choose(t, part):
                n, tn = ORDER.index(t), TILES[t][1]
                half = slice(64 * part, 64 * part + 64)
                act.wait_ge(sc_s, 2 * n + part + 1)
                S.activation(gts[0:tn, n % 2, half], gts[0:tn, n % 2, half], ACT.Exp).then_inc(sce_s, 1)

            def do_fold():
                n = ORDER.index(0)
                act.wait_ge(idx_s, 2 * n + 2)
                act.dma_start(idxf[0:64, :], idx[0:64, n % 2, 0:64]).then_inc(fold_in, 16)
                act.dma_start(idxf[64:128, :], idx[0:64, n % 2, 64:128]).then_inc(fold_in, 16)
                act.dma_start(gtf[0:64, :], gts[0:64, n % 2, 0:64]).then_inc(fold_in, 16)
                act.dma_start(gtf[64:128, :], gts[0:64, n % 2, 64:128]).then_inc(fold_in, 16)
                act.dma_start(x1[0][64:128, :], x1[0][0:64, :]).then_inc(fold_in, 16)

            done = [0]

            diag_slot = []

            def diagonals(t, c):
                n, tn, base = ORDER.index(t), TILES[t][1], slot_base[t]
                eye = s("fold") if t == 0 else ident
                done[0] += 1
                act.wait_ge(a_s, done[0])
                for k in range(STEP_SLOTS * c, STEP_SLOTS * c + STEP_SLOTS):
                    q = base + k
                    if on_dve[q]:
                        continue
                    d = q - by_dve[q]
                    if d >= DIAGS:
                        act.wait_ge(v_used, by_pe[diag_slot[d - DIAGS]])
                    diag_slot.append(q)
                    S.activation(diag[:, d % DIAGS, 0:tn], eye, ACT.Copy, scale=aact[:, n % 2, k:k + 1]).then_inc(diag_s, 1)

            def do_peer(t, c):
                n, base = ORDER.index(t), slot_base[t]
                act.wait_ge(dots, base + STEP_SLOTS * c + STEP_SLOTS)
                k = slice(STEP_SLOTS * c, STEP_SLOTS * c + STEP_SLOTS)
                S.activation(hact[:, n % 2, k], hdot[:, n % 2, k], ACT.Gelu).then_inc(act_s, 1)

            def do_before(t, c):
                if c:
                    diagonals(t, c - 1)

            def do_last(t):
                diagonals(t, n_slots(t) // STEP_SLOTS - 1)

            def do_final(t):
                t0, tn = TILES[t]
                deviation(tn)
                act.wait_ge(y_s, ORDER.index(t) + 1)
                act.dma_start(io["y"][t0:t0 + tn, :], x1[t][0:tn, :]).then_inc(y_out, 16)

            here = {"tables": do_tables, "u": do_u, "ut": do_ut, "uc": do_uc, "wt": do_wt, "k": do_k, "ws": do_ws, "y": do_y, "ht": do_ht,
                    "turn": do_turn, "ss": do_ss, "pvs": do_pvs, "s": do_s, "pv": do_pv, "gates": do_gates, "merge": do_merge,
                    "wo": do_wo, "xt": do_xt, "wq": do_wq, "choose": do_choose, "fold": do_fold, "before": do_before, "peer": do_peer, "last": do_last,
                    "final": do_final}
            for item in mixer_first(plan.items):
                if item[0] in here:
                    here[item[0]](*item[1:])
            act.wait_ge(y_out, 16 * 5)
            act.wait_ge(kv_out, 16 * 4)
            act.wait_ge(ssm_out, 16)
            act.wait_ge(win_out, 16 * 2)


def packed_inputs(I):
    f = lambda n: np.asarray(I[n])[0]
    x = np.concatenate([np.asarray(I["x_sample"]).reshape(64, DM), np.asarray(I["x_prompt"]).reshape(SEQ, DM)])
    order = [kv * HP + hp for hp in range(HP) for kv in range(NKV)]
    w_in, b_in = f("w_in"), f("b_in")
    wu, wq, wkv, wgs, wga = np.split(w_in, [512, 1024, 1280, 2304], axis=1)
    bu, bq, bkv, bgs, bga = np.split(b_in, [512, 1024, 1280, 2304])
    wq = wq.reshape(DM, NH, HD)[:, order].reshape(DM, 512)
    bq = bq.reshape(NH, HD)[order].reshape(512)
    kmaj = lambda w: w.reshape(-1, 128, w.shape[1]).transpose(1, 0, 2)
    wu, wq, wkv, wgs, wga = (kmaj(w) for w in (wu, wq, wkv, wgs, wga))
    glu, up = kmaj(f("w_glu")), kmaj(f("w_attn_up").reshape(NH, HD, DM)[order].reshape(512, DM))
    wo, wpq = kmaj(f("w_out")), kmaj(f("peer_wq"))
    cols = lambda w, m: w[:, :, 128 * m:128 * m + 128]
    cut = {"u": lambda i: cols(wu, i), "q": lambda i: wq[:, 2 * i:2 * i + 2], "kv": lambda i: wkv[:, 4 * i:4 * i + 4],
           "gs": lambda i: cols(wgs, i), "ga": lambda i: cols(wga, i),
           "glu": lambda i: np.concatenate([cols(glu, i), cols(glu, 8 + i)], 1),
           "up": lambda i: np.concatenate([cols(up, 2 * i), cols(up, 2 * i + 1)], 1),
           "wo": lambda i: wo[:, i], "wq": lambda i: cols(wpq, i)}
    w = np.stack([cut[k](i).reshape(128, 1024) for _, k, i in Plan().pieces])

    def pairs(a):
        a = a.reshape(GP, 2, NS, *a.shape[2:])
        return np.moveaxis(a, 0, 2).reshape(128, GP, *a.shape[3:])

    freqs = np.float32(500000.0) ** (-np.arange(0, ROPE, 2, dtype=np.float32) / np.float32(ROPE))
    pos = np.concatenate([np.tile(PAST + np.arange(STEP), NSEQ), np.arange(SEQ)]).astype(np.float32)
    ang = (pos[:, None] * freqs[None, :]).astype(np.float32)
    tab = np.stack([np.cos(ang.astype(np.float64)), np.sin(ang.astype(np.float64))], 1).astype(np.float32)
    rope = np.zeros((128, 5, 2, 8), np.float32)
    for t, (t0, tn) in enumerate(TILES):
        rope[:tn, t] = tab[t0:t0 + tn]
    q, k = np.arange(128)[:, None], np.arange(256)[None, :]
    maskp = np.where((128 + q - k >= 0) & (128 + q - k < WIN), 0.0, NEG).astype(np.float32)
    masks = np.full((128, 2, WIN + 64), NEG, np.float32)
    row = np.arange(128)
    for hf in range(2):
        b, st = 4 * hf + row // 32, row % 8
        masks[:, hf, :WIN][st[:, None] < np.arange(WIN)[None, :]] = 0.0
        new = np.arange(64)[None, :]
        masks[:, hf, WIN:][(new // 8 == b[:, None]) & (new % 8 <= st[:, None])] = 0.0
    rep = lambda v: np.broadcast_to(v, (128, v.size))
    per = lambda v: v.reshape(-1, 128).T
    sinks = f("attn_sinks")
    sink_rows = np.stack([sinks[4 * kv + (row // 8) % 4] for kv in range(2)], 1)
    re, im = (np.asarray(I[n])[0].transpose(1, 2, 0) for n in ("state_ssm_re", "state_ssm_im"))
    dsk = np.zeros((128, G * GC), np.float32)
    parts = {
        "ident": np.eye(128, dtype=np.float32), "fold": np.tile(np.eye(64, dtype=np.float32), (2, 1)),
        "are": pairs(f("ssm_a_re")), "aim": pairs(f("ssm_a_im")),
        "ldt": pairs(np.broadcast_to(f("ssm_log_dt")[:, None], (G, NS))),
        "bb": np.stack([pairs(f("ssm_b_re")), pairs(f("ssm_b_im"))], 1),
        "cc": np.stack([pairs(f("ssm_c_re").transpose(0, 2, 1)), pairs(f("ssm_c_im").transpose(0, 2, 1))], 1),
        "k12": np.concatenate([f("peer_k1").transpose(2, 0, 1), f("peer_k2").transpose(2, 0, 1)]),
        "maskp": maskp, "masks": masks, "rope": rope, "h0": np.stack([pairs(re), pairs(im)], 1),
        "bu": per(bu), "bgs": per(bgs), "bga": per(bga), "bglu": per(f("b_glu")),
        "sinkp": rep(sinks), "sinks": sink_rows, "dskip": rep(f("ssm_d")), "iota": rep(np.arange(TOPK, dtype=np.float32)),
        "bqkv": rep(np.concatenate([bq, bkv])),
    }
    small = np.concatenate([np.ascontiguousarray(parts[n]).reshape(128, wd) for n, wd in _SMALL], 1)
    ck, cv = np.asarray(I["cache_k_win"])[0], np.asarray(I["cache_v_win"])[0]
    lnp = np.concatenate([rep(f(n)) for n in ("ln1_g", "ln1_b", "ln2_g", "ln2_b")], 1)
    out = {"small": small, "xT": x.T, "x": x, "w": w, "lnp": lnp,
           "kcT": ck.transpose(2, 3, 0, 1).reshape(128, NSEQ, WIN), "vc": cv.transpose(1, 0, 2, 3).reshape(WIN, NSEQ, 128),
           "ckn": ck.reshape(NSEQ, WIN, 128), "cvn": cv.reshape(NSEQ, WIN, 128), "pu": f("peer_u"), "pv": f("peer_v")}
    return {k: np.ascontiguousarray(v) for k, v in out.items()}


OUTS = {"y": (TOK, DM), "kwp": (WIN, 128), "vwp": (WIN, 128), "kws": (NSEQ, WIN, 128), "vws": (NSEQ, WIN, 128),
        "ssm": (128, 2 * GP * (1 + NSEQ))}


def kernel(**inputs):
    import concourse.bacc as bacc
    from concourse.bass_utils import run_bass_kernel_spmd

    nc = bacc.Bacc("TRN2", target_bir_lowering=False, num_devices=1)
    arrays, io = {}, {}
    for name, a in packed_inputs(inputs).items():
        arrays["in_" + name] = a
        io[name] = nc.dram_tensor("in_" + name, a.shape, mybir.dt.from_np(a.dtype), kind="ExternalInput").ap()
    for name, shape in OUTS.items():
        io[name] = nc.dram_tensor("out_" + name, shape, F32, kind="ExternalOutput").ap()
    hybrid_step(nc, io)
    r = run_bass_kernel_spmd(nc, [arrays], core_ids=[0]).results[0]
    y = r["out_y"]
    ssm = r["out_ssm"].reshape(2, NS, 2, GP, 1 + NSEQ).transpose(2, 4, 3, 0, 1).reshape(2, 1 + NSEQ, G, NS)
    win = lambda n, b: r["out_" + n].reshape(1, b, WIN, NKV, HD)
    return (y[64:].reshape(1, SEQ, DM), y[:64].reshape(NSEQ, STEP, DM), win("kwp", 1), win("vwp", 1),
            ssm[0:1, 0:1], ssm[1:2, 0:1], win("kws", NSEQ), win("vws", NSEQ), ssm[0:1, 1:], ssm[1:2, 1:])
```
